# Optimizing a Trainium2 kernel written in Bass

```python
import math
import jax, jax.numpy as jnp
from jax import lax
import numpy as np

D_MODEL = 2048
BATCH = 1
SEQ = 256
DEPTH = 1
DEC_BATCH = 8
DEC_SEQ = 1
PAST_LEN = 2048
PAGE_SIZE = 128

HEAD_DIM = 64
D_INNER = 2 * D_MODEL
N_HEADS = D_INNER // HEAD_DIM
N_GROUPS = 8
D_STATE = 128
CONV_K = 4
CONV_DIM = D_INNER + 2 * N_GROUPS * D_STATE
CHUNK = 128
D_POOL = D_MODEL
POOL_WINDOWS = (2, 4, 8, 16)
POOL_GROUPS = len(POOL_WINDOWS)
POOL_GC = D_POOL // POOL_GROUPS
POOL_BUF = max(POOL_WINDOWS) - 1
D_FF = 5504
FFN_K = 3
D_IN_TOTAL = D_INNER + CONV_DIM + N_HEADS + D_POOL + 2 * D_MODEL
IN_SPLITS = (D_INNER, D_INNER + CONV_DIM, D_INNER + CONV_DIM + N_HEADS,
             D_INNER + CONV_DIM + N_HEADS + D_POOL)
ALPHA = (2 * DEPTH) ** 0.25
BETA = (8 * DEPTH) ** -0.25
LN_EPS = 1e-5
RMS_EPS = 1e-5

kernel_name = "ssd_pool_gated_hybrid_deepnorm_step"

def layer_norm(x, g, b):
    xf = x.astype(jnp.float32)
    mu = jnp.mean(xf, axis=-1, keepdims=True)
    var = jnp.mean(jnp.square(xf - mu), axis=-1, keepdims=True)
    y = (xf - mu) * lax.rsqrt(var + LN_EPS) * g.astype(jnp.float32) + b.astype(jnp.float32)
    return y.astype(x.dtype)

def gated_rmsnorm(y, z, w):
    v = y.astype(jnp.float32) * jax.nn.silu(z.astype(jnp.float32))
    shp = v.shape
    v = v.reshape(shp[:-1] + (N_GROUPS, shp[-1] // N_GROUPS))
    v = v * lax.rsqrt(jnp.mean(jnp.square(v), axis=-1, keepdims=True) + RMS_EPS)
    return v.reshape(shp) * w.astype(jnp.float32)

def causal_dwconv(u, buf, w, b):
    k = w.shape[0]
    l = u.shape[1]
    ext = jnp.concatenate([buf.astype(u.dtype), u], axis=1)
    y = b
    for j in range(k):
        y = y + ext[:, j:j + l] * w[j]
    return y, ext[:, -(k - 1):]

def ssd_scan(xs, dt, a, bm, cm, s0):
    bsz, l, h, p = xs.shape
    g, n = bm.shape[2], bm.shape[3]
    r = h // g
    q = min(CHUNK, l)
    nc = -(-l // q)
    pad = nc * q - l
    if pad:
        pw4 = ((0, 0), (0, pad), (0, 0), (0, 0))
        xs = jnp.pad(xs, pw4)
        bm = jnp.pad(bm, pw4)
        cm = jnp.pad(cm, pw4)
        dt = jnp.pad(dt, ((0, 0), (0, pad), (0, 0)))
    xs = xs.astype(jnp.float32).reshape(bsz, nc, q, g, r, p)
    dt = dt.reshape(bsz, nc, q, g, r)
    bm = bm.astype(jnp.float32).reshape(bsz, nc, q, g, n)
    cm = cm.astype(jnp.float32).reshape(bsz, nc, q, g, n)
    a_cum = jnp.cumsum(dt * a.reshape(g, r), axis=2)
    xdt = xs * dt[..., None]
    causal = jnp.tril(jnp.ones((q, q), dtype=bool))[:, :, None, None]
    seg = a_cum[:, :, :, None] - a_cum[:, :, None]
    decay = jnp.where(causal, jnp.exp(jnp.where(causal, seg, 0.0)), 0.0)
    cb = jnp.einsum('bcign,bcjgn->bcijg', cm, bm)
    y_diag = jnp.einsum('bcijgr,bcjgrp->bcigrp', cb[..., None] * decay, xdt)
    end_decay = jnp.exp(a_cum[:, :, -1:] - a_cum)
    chunk_states = jnp.einsum('bcjgn,bcjgrp->bcgrpn', bm, xdt * end_decay[..., None])
    chunk_decay = jnp.exp(a_cum[:, :, -1])

    def step(s, inp):
        st, dc = inp
        return s * dc[..., None, None] + st, s

    s_init = s0.astype(jnp.float32).reshape(bsz, g, r, p, n)
    s_final, s_prev = lax.scan(step, s_init,
                               (jnp.moveaxis(chunk_states, 1, 0), jnp.moveaxis(chunk_decay, 1, 0)))
    s_prev = jnp.moveaxis(s_prev, 0, 1)
    y_off = jnp.einsum('bcign,bcgrpn->bcigrp', cm, s_prev) * jnp.exp(a_cum)[..., None]
    y = (y_diag + y_off).reshape(bsz, nc * q, h, p)[:, :l]
    return y, s_final.reshape(bsz, h, p, n)

def pool_mix(u, buf, start_pos, w_pool, scale):
    bsz, l, c = u.shape
    pb = buf.shape[1]
    ext = jnp.concatenate([buf.astype(u.dtype), u], axis=1)
    cs = jnp.concatenate([jnp.zeros((bsz, 1, c), jnp.float32),
                          jnp.cumsum(ext.astype(jnp.float32), axis=1)], axis=1)
    end = cs[:, pb + 1:]
    pos = start_pos + jnp.arange(l)
    means = []
    for gi, win in enumerate(POOL_WINDOWS):
        sl = slice(gi * POOL_GC, (gi + 1) * POOL_GC)
        win_sum = end[..., sl] - cs[:, pb + 1 - win: pb + 1 - win + l, sl]
        cnt = jnp.minimum(win, pos + 1).astype(jnp.float32)
        means.append(win_sum / cnt[None, :, None])
    pooled = jnp.concatenate(means, axis=-1) - u.astype(jnp.float32)
    pooled = pooled.reshape(bsz, l, POOL_GROUPS, POOL_GC)
    out = jnp.einsum('blgc,gcd->blgd', pooled, w_pool.astype(jnp.float32)).reshape(bsz, l, c)
    out = out * scale.astype(jnp.float32)
    return out.astype(u.dtype), ext[:, -pb:]

def layer(x, s_ssm, s_conv, s_pool, s_ffn, start_pos, lw):
    (w_in, b_gate, conv_w, conv_b, dt_bias, a_log, d_skip, norm_w, w_br, w_pool, pool_scale,
     w_out, ln1_g, ln1_b, w_up, fconv_w, fconv_b, w_down, ln2_g, ln2_b) = lw
    bsz, l, _ = x.shape
    proj = x @ w_in
    z, xbc, dt_raw, pool_in, gate_raw = jnp.split(proj, IN_SPLITS, axis=-1)
    xbc, new_conv = causal_dwconv(xbc, s_conv, conv_w, conv_b)
    xbc = jax.nn.silu(xbc)
    xs, bm, cm = jnp.split(xbc, (D_INNER, D_INNER + N_GROUPS * D_STATE), axis=-1)
    xs = xs.reshape(bsz, l, N_HEADS, HEAD_DIM)
    bm = bm.reshape(bsz, l, N_GROUPS, D_STATE)
    cm = cm.reshape(bsz, l, N_GROUPS, D_STATE)
    dt = jax.nn.softplus(dt_raw.astype(jnp.float32) + dt_bias.astype(jnp.float32))
    a = -jnp.exp(a_log.astype(jnp.float32))
    y, new_ssm = ssd_scan(xs, dt, a, bm, cm, s_ssm)
    y = y + d_skip.astype(jnp.float32)[:, None] * xs.astype(jnp.float32)
    y = gated_rmsnorm(y.reshape(bsz, l, D_INNER), z, norm_w).astype(x.dtype)
    y_a = y @ w_br
    y_b, new_pool = pool_mix(pool_in, s_pool, start_pos, w_pool, pool_scale)
    g_a, g_b = jnp.split(jax.nn.sigmoid(gate_raw + b_gate), 2, axis=-1)
    mix = (g_a * y_a + g_b * y_b) @ w_out
    x1 = layer_norm(ALPHA * x + mix, ln1_g, ln1_b)
    h, new_ffn = causal_dwconv(x1 @ w_up, s_ffn, fconv_w, fconv_b)
    hg, hv = jnp.split(h, 2, axis=-1)
    x2 = layer_norm(ALPHA * x1 + (jax.nn.silu(hg) * hv) @ w_down, ln2_g, ln2_b)
    return x2, new_ssm.astype(x.dtype), new_conv, new_pool, new_ffn

def setup_inputs(seed: int = 0) -> dict:
    key = jax.random.key(seed)
    ks = jax.random.split(key, 32)
    f32 = jnp.float32
    nrm = lambda k, shp, s: jax.random.normal(k, shp, f32) * s
    dt0 = jnp.exp(jax.random.uniform(ks[10], (DEPTH, N_HEADS), f32)
                  * (math.log(0.1) - math.log(0.001)) + math.log(0.001))
    return {
        "x_prompt": nrm(ks[0], (BATCH, SEQ, D_MODEL), 1.0),
        "x_sample": nrm(ks[1], (DEC_BATCH, DEC_SEQ, D_MODEL), 1.0),
        "state_ssm": nrm(ks[2], (DEPTH, DEC_BATCH, N_HEADS, HEAD_DIM, D_STATE), 0.1),
        "state_ssd_conv": nrm(ks[3], (DEPTH, DEC_BATCH, CONV_K - 1, CONV_DIM), 1.0),
        "state_pool": nrm(ks[4], (DEPTH, DEC_BATCH, POOL_BUF, D_POOL), 1.0),
        "state_ffn_conv": nrm(ks[5], (DEPTH, DEC_BATCH, FFN_K - 1, 2 * D_FF), 1.0),
        "w_in": nrm(ks[6], (DEPTH, D_MODEL, D_IN_TOTAL), D_MODEL ** -0.5),
        "b_gate": nrm(ks[7], (DEPTH, 2 * D_MODEL), 0.02),
        "conv_w": nrm(ks[8], (DEPTH, CONV_K, CONV_DIM), CONV_K ** -0.5),
        "conv_b": nrm(ks[9], (DEPTH, CONV_DIM), 0.02),
        "dt_bias": jnp.log(jnp.expm1(dt0)),
        "a_log": jnp.log(jax.random.uniform(ks[11], (DEPTH, N_HEADS), f32, 1.0, 16.0)),
        "d_skip": 1.0 + nrm(ks[12], (DEPTH, N_HEADS), 0.02),
        "ssd_norm_w": 1.0 + nrm(ks[13], (DEPTH, D_INNER), 0.02),
        "w_ssd_branch": nrm(ks[14], (DEPTH, D_INNER, D_MODEL), D_INNER ** -0.5),
        "w_pool": nrm(ks[15], (DEPTH, POOL_GROUPS, POOL_GC, POOL_GC), POOL_GC ** -0.5),
        "pool_scale": 1.0 + nrm(ks[16], (DEPTH, D_POOL), 0.1),
        "w_out": nrm(ks[17], (DEPTH, D_MODEL, D_MODEL), BETA * D_MODEL ** -0.5),
        "ln1_g": 1.0 + nrm(ks[18], (DEPTH, D_MODEL), 0.02),
        "ln1_b": nrm(ks[19], (DEPTH, D_MODEL), 0.02),
        "w_up": nrm(ks[20], (DEPTH, D_MODEL, 2 * D_FF), D_MODEL ** -0.5),
        "ffn_conv_w": nrm(ks[21], (DEPTH, FFN_K, 2 * D_FF), FFN_K ** -0.5),
        "ffn_conv_b": nrm(ks[22], (DEPTH, 2 * D_FF), 0.02),
        "w_down": nrm(ks[23], (DEPTH, D_FF, D_MODEL), BETA * D_FF ** -0.5),
        "ln2_g": 1.0 + nrm(ks[24], (DEPTH, D_MODEL), 0.02),
        "ln2_b": nrm(ks[25], (DEPTH, D_MODEL), 0.02),
    }

def reference(x_prompt, x_sample, state_ssm, state_ssd_conv, state_pool, state_ffn_conv,
              w_in, b_gate, conv_w, conv_b, dt_bias, a_log, d_skip, ssd_norm_w, w_ssd_branch,
              w_pool, pool_scale, w_out, ln1_g, ln1_b, w_up, ffn_conv_w, ffn_conv_b, w_down,
              ln2_g, ln2_b):
    yp, ys = x_prompt, x_sample
    bp = x_prompt.shape[0]
    dtp = x_prompt.dtype
    p_ssm, p_conv, p_pool, p_ffn = [], [], [], []
    s_ssm, s_conv, s_pool, s_ffn = [], [], [], []
    for i in range(DEPTH):
        lw = (w_in[i], b_gate[i], conv_w[i], conv_b[i], dt_bias[i], a_log[i], d_skip[i],
              ssd_norm_w[i], w_ssd_branch[i], w_pool[i], pool_scale[i], w_out[i],
              ln1_g[i], ln1_b[i], w_up[i], ffn_conv_w[i], ffn_conv_b[i], w_down[i],
              ln2_g[i], ln2_b[i])
        yp, a1, a2, a3, a4 = layer(
            yp,
            jnp.zeros((bp, N_HEADS, HEAD_DIM, D_STATE), dtp),
            jnp.zeros((bp, CONV_K - 1, CONV_DIM), dtp),
            jnp.zeros((bp, POOL_BUF, D_POOL), dtp),
            jnp.zeros((bp, FFN_K - 1, 2 * D_FF), dtp),
            0, lw)
        ys, b1, b2, b3, b4 = layer(ys, state_ssm[i], state_ssd_conv[i], state_pool[i],
                                   state_ffn_conv[i], PAST_LEN, lw)
        p_ssm.append(a1); p_conv.append(a2); p_pool.append(a3); p_ffn.append(a4)
        s_ssm.append(b1); s_conv.append(b2); s_pool.append(b3); s_ffn.append(b4)
    return (yp, ys,
            jnp.stack(p_ssm), jnp.stack(p_conv), jnp.stack(p_pool), jnp.stack(p_ffn),
            jnp.stack(s_ssm), jnp.stack(s_conv), jnp.stack(s_pool), jnp.stack(s_ffn))


_drawn_inputs = setup_inputs


def setup_inputs(seed=0):
    import zlib

    import numpy as np

    out = dict(_drawn_inputs(seed))
    spreads = {}
    factors = {'b_gate': 8.0,
     'd_skip': 86.892,
     'ssd_norm_w': 22.881,
     'ln1_g': 2.723,
     'ln1_b': 2.785,
     'ffn_conv_b': 6.874,
     'ln2_g': 22.763,
     'ln2_b': 21.841,
     'pool_scale': 4.806}
    for name, (base, spread) in spreads.items():
        noise = np.random.default_rng([zlib.crc32(name.encode()), seed]).standard_normal(out[name].shape)
        drawn = base * np.exp(spread * noise) if base else spread * noise
        out[name] = __import__('jax').numpy.asarray(drawn.astype(out[name].dtype))
    for name, factor in factors.items():
        out[name] = (out[name] * factor).astype(out[name].dtype)
    return out
```

```python
from contextlib import ExitStack

import numpy as np

import concourse.bass as bass
from concourse import mybir

F32 = mybir.dt.float32
F32R = mybir.dt.float32r
ACT = mybir.ActivationFunctionType
ALU = mybir.AluOpType
AX_X = mybir.AxisListType.X

P = 128
D_MODEL = 2048
SEQ = 256
NS = 8
T = SEQ + NS
D_INNER = 2 * D_MODEL
HEAD_DIM = 64
N_HEADS = D_INNER // HEAD_DIM
G = 8
D_STATE = 128
CONV_K = 4
CHUNK = 128
WINDOWS = (2, 4, 8, 16)
POOL_BUF = max(WINDOWS) - 1
D_FF = 5504
FFN_K = 3
ALPHA = 2.0 ** 0.25
EPS = 1e-5

KT = D_MODEL // P
GT = D_INNER // G // P
HG = N_HEADS // G
JF = D_FF // P
CT = 2 + GT
UW = CONV_K - 1 + SEQ + NS * CONV_K
CVW = UW - (CONV_K - 1)
PW = 16 + T
FW = FFN_K - 1 + SEQ + NS * FFN_K
FCW = FW - (FFN_K - 1)
HT = 8
RING = 4
EW = 2 * NS + 2 + CHUNK

C_CONV = 0
C_NORM = C_CONV + G * CT * 5
C_GATE = C_NORM + G * GT
C_PSC = C_GATE + 2 * KT
C_LN = C_PSC + KT
C_FC = C_LN + 4 * KT
C_HEAD = C_FC + JF * 2 * 4
N_PAR = C_HEAD + 3
K_ID, K_TRI, K_LOW, K_ONE, K_E = 0, P, 2 * P, 3 * P, 4 * P
K_MASK = K_E + GT * P
K_RC = K_MASK + G
N_CON = K_RC + 16


def wait(e, sem, value):
    if not (isinstance(value, int) and value <= 0):
        e.wait_ge(sem, value)



def bass_hybrid_layer(nc, A, O):
    ctx = ExitStack()
    with ctx:
        def sem(name):
            return ctx.enter_context(nc.semaphore(name))

        place = [(nc.sbuf_base + 63) // 64 * 64]

        def sb(name, shape, dt=F32):
            offset = place[0]
            place[0] += (int(np.prod(shape)) * 4 + 31) // 32 * 32
            assert place[0] <= nc.sbuf_usable_end, (name, place[0], nc.sbuf_usable_end)
            return nc.alloc_sbuf_tensor_at(name, [P, *shape], dt, offset=offset).ap()

        raw = sb("w_raw", [RING, HT * P])
        whi = sb("w_hi", [RING, HT * P], F32R)
        wlo = sb("w_lo", [RING, HT * P], F32R)
        con = sb("constants", [N_CON])
        par = sb("params", [N_PAR])
        rsum = sb("row_sum", [T])
        ident, tri, low, ones = (con[:, k:k + P] for k in (K_ID, K_TRI, K_LOW, K_ONE))
        conv_w = par[:, C_CONV:C_NORM].rearrange("p (g s k) -> p g s k", g=G, s=CT)
        norm_w = par[:, C_NORM:C_GATE].rearrange("p (g t) -> p g t", g=G)
        fc_w = par[:, C_FC:C_HEAD].rearrange("p (j w k) -> p j w k", j=JF, w=2)

        arena = place[0]
        xhi = sb("x_hi", [KT, T], F32R)
        xlo = sb("x_lo", [KT, T], F32R)
        ya = sb("branch_a", [KT, T])
        poolu = sb("pool_in", [KT, PW])

        staging = place[0]
        u6 = sb("conv_in", [CT, UW])
        xbc = sb("xbc", [CT, CVW])
        scb = sb("conv_rows_s", [G, CT, NS, 3])
        cpo = sb("conv_rows_p", [G, CT, 3])
        diag = sb("pe_right", [4, P])
        dec = sb("decay", [4, 4, P])
        cbm = sb("cb_masked", [2, P])
        btok = sb("b_tok", [2, P])
        xdt = sb("xdt", [2, GT * P])
        xde = sb("xdt_end", [2, GT * P])
        s0 = sb("state_0", [GT * P])
        s1 = sb("state_1", [GT * P])
        at_bc = place[0]
        bc = sb("bc_rows", [4, 4, P])
        st = sb("state_s", [2, 2, GT, P])
        tm = sb("state_add", [2, GT, P])
        ty = sb("state_c", [2, GT, P])
        exps = sb("per_channel", [GT, EW])
        exr = sb("per_head", [EW])
        exg = sb("per_head_group", [EW])
        dx = sb("dt_x", [NS, GT])
        zs = sb("z_silu", [GT, T])
        yt = sb("y", [GT, T])
        y3 = sb("y_normed", [GT, T])
        yhi = sb("y_hi", [GT, T], F32R)
        ylo = sb("y_lo", [GT, T], F32R)
        rs = sb("rstd", [2, T])
        tok = sb("per_token", [4, N_HEADS])
        acs = sb("a_cum", [2, N_HEADS])
        fe = sb("dt_end", [2, N_HEADS])
        ctot = sb("decay_total", [2, N_HEADS])
        hcol = sb("head_cols", [2])
        sml = sb("small_d", [2, GT, NS])
        place[0] = at_bc
        dts = sb("dt_steps", [7, T])

        place[0] = staging
        mhi = sb("mix_hi", [KT, T], F32R)
        mlo = sb("mix_lo", [KT, T], F32R)
        spb = sb("pool_rows_s", [KT, NS, 16])
        ppo = sb("pool_rows_p", [KT, POOL_BUF])
        pa = sb("pool_a", [4, 16 + SEQ])
        pb = sb("pool_b", [4, 16 + SEQ])
        pp = sb("pooled", [4, T])
        psm = sb("pool_small", [4, 16 + NS])
        phi = sb("pooled_hi", [2, 4, T], F32R)
        plo = sb("pooled_lo", [2, 4, T], F32R)
        yb = sb("branch_b", [KT, T])
        sg = sb("gate_sig", [4, T])
        mx = sb("mix_parts", [2, 2, T])

        place[0] = arena
        hhi = sb("h_hi", [JF, T], F32R)
        hlo = sb("h_lo", [JF, T], F32R)
        x1hi = sb("x1_hi", [KT, T], F32R)
        x1lo = sb("x1_lo", [KT, T], F32R)
        res = sb("residual", [KT, T])
        uf = sb("ffn_in", [2, FW])
        fc = sb("ffn_conv", [2, FCW])
        hh = sb("ffn_gated", [T])
        sfb = sb("ffn_rows_s", [JF, 2, NS, 2])
        fpo = sb("ffn_rows_p", [JF, 2, 2])
        lnr = sb("ln_rows", [4, T])
        lsq = sb("ln_squares", [2, 4, T])

        acc = [ctx.enter_context(nc.psum_tensor(f"acc{i}", [P, 512], F32)) for i in range(4)]
        seg_b, tp_b, yd_b, misc = (ctx.enter_context(nc.psum_tensor(n, [P, 512], F32))
                                   for n in ("seg", "turned", "y_heads", "misc"))

        raw_landed = [sem(f"raw_landed{i}") for i in range(RING)]
        hi_ready, lo_ready, half_used = sem("hi_ready"), sem("lo_ready"), sem("half_used")
        acc_act, acc_dve = sem("acc_act"), sem("acc_dve")
        con_in, par_in, scb_in, x_in = sem("con_in"), sem("par_in"), sem("scb_in"), [sem(f"x_in{i}") for i in range(4)]
        spb_in, sfb_in = sem("spb_in"), sem("sfb_in")
        st_in, st_out = [sem(f"st_in{i}") for i in range(2)], [sem(f"st_out{i}") for i in range(2)]
        xhi_ready, xlo_ready, zeroed = sem("xhi_ready"), sem("xlo_ready"), sem("zeroed")
        dt_act, dt_mm, dt_dve = sem("dt_act"), sem("dt_mm"), sem("dt_dve")
        exr_ready, exp_mm, exps_ready = sem("exr_ready"), sem("exp_mm"), sem("exps_ready")
        ubuf_ready, conv_done, ust_done = sem("ubuf_ready"), sem("conv_done"), sem("ust_done")
        xbc_ready = sem("xbc_ready")
        t_ready, seg_mm, dec_ready, m_ready = sem("t_ready"), sem("seg_mm"), sem("dec_ready"), sem("m_ready")
        dg_ready, bc_mm, bc_ready = sem("dg_ready"), sem("bc_mm"), sem("bc_ready")
        cb_mm, cbm_ready, btok_ready = sem("cb_mm"), sem("cbm_ready"), sem("btok_ready")
        xt_mm, xdt_ready = sem("xt_mm"), sem("xdt_ready")
        st_mm, s0_ready, st1_ready, s1_out = sem("st_mm"), sem("s0_ready"), sem("st1_ready"), sem("s1_out")
        yd_mm, yd_read, yo_mm, yo_read = sem("yd_mm"), sem("yd_read"), sem("yo_mm"), sem("yo_read")
        pool_step, snew, ty_ready, red_done = sem("pool_step"), sem("snew"), sem("ty_ready"), sem("red_done")
        dve_step = sem("dve_step")
        vsq_ready, ssq_mm, ms_ready, std_ready = sem("vsq_ready"), sem("ssq_mm"), sem("ms_ready"), sem("std_ready")
        rstd_ready, y3_ready, yhi_ready, ylo_ready = sem("rstd_ready"), sem("y3_ready"), sem("yhi_ready"), sem("ylo_ready")
        pooled, phi_ready, plo_ready, pool_rows = sem("pooled"), sem("phi_ready"), sem("plo_ready"), sem("pool_rows")
        yb_ready, mx_step, mx_ready, mhi_ready, mlo_ready = (sem("yb_ready"), sem("mx_step"), sem("mx_ready"),
                                                             sem("mhi_ready"), sem("mlo_ready"))
        res_step, res_ready, rsum_done, mean_mm, mu_ready = (sem("res_step"), sem("res_ready"), sem("rsum_done"),
                                                             sem("mean_mm"), sem("mu_ready"))
        rc_ready, sq_ready, sq_mm, var_ready, lnstd, lnr_ready = (sem("rc_ready"), sem("sq_ready"), sem("sq_mm"),
                                                                  sem("var_ready"), sem("lnstd"), sem("lnr_ready"))
        norm_step, ln_ready, x1hi_ready, x1lo_ready = (sem("norm_step"), sem("ln_ready"), sem("x1hi_ready"),
                                                       sem("x1lo_ready"))
        fbuf_ready, fconv, fst_done, fsilu, fh_ready, fhi_ready, flo_ready = (
            sem("fbuf_ready"), sem("fconv"), sem("fst_done"), sem("fsilu"), sem("fh_ready"), sem("fhi_ready"),
            sem("flo_ready"))
        conv_out, pool_out, stored = sem("conv_out"), sem("pool_out"), sem("stored")

        FIRST_HALF = 2
        PLAIN = [("s", i) for i in range(CT)] + [("z", i) for i in range(GT)] + [("p", 0), ("p", 1)]
        WITH_W = PLAIN[:CT] + [("w", i) for i in range(GT)] + PLAIN[CT:]
        ALL = WITH_W
        DT_DONE, DT_TOK, DT_ACT = 20, 21, 6
        ACT_POOL, ACT_GATE, ACT_UP = 12 * G, 12 * G + KT, 12 * G + KT + 2 * KT
        DVE_OUT, DVE_DOWN = GT * GT * G, GT * GT * G + KT
        Q_TAIL, Q_POOL, Q_GATE, Q_OUT, Q_UP, Q_DOWN = 62, 64, 66, 82, 90, 133
        DOWN_TILES = [8, 7, 7, 7, 7, 7]
        N_HALVES = 4 * (Q_DOWN + 24) + 2

        def q_of(g, lag):
            return 8 * g - 2 if lag else 0

        def slots(lag):
            off, out = FIRST_HALF, []
            for kind, i in ALL:
                if kind == "w" and not lag:
                    out.append((kind, i, None))
                else:
                    out.append((kind, i, off))
                    off += 2
            return out

        def prompt_and_rows(u, s):
            return u[:, s, CONV_K - 1 + SEQ:UW].rearrange("p (b f) -> p b f", f=CONV_K)

        u_rows = u6[:, :, CONV_K - 1 + SEQ:UW].rearrange("p s (b f) -> p s b f", f=CONV_K)
        xbc_s = xbc[:, :, SEQ:CVW].rearrange("p s (b f) -> p s b f", f=CONV_K)[:, :, :, CONV_K - 1]
        seg_v = seg_b[:, :].rearrange("p (h i) -> p h i", h=4)
        dec_f = dec.rearrange("p u h i -> p u (h i)")
        diag_f = diag.rearrange("p h i -> p (h i)")
        bc_f = bc.rearrange("p i b n -> p i (b n)")

        block = ctx.enter_context(nc.Block())

        @block.sync
        def _(sp):
            def load(src, q, off, tiles=HT):
                wait(sp, lo_ready, 4 * q + off - RING + 1)
                sp.dma_start(raw[:, off % RING, 0:tiles * P], src).then_inc(raw_landed[off % RING], 16)

            def slab(src, q, off):
                load(src[:, 0:HT * P], q, off)
                load(src[:, HT * P:2 * HT * P], q, off + 1)

            def iteration(g, lag):
                q = q_of(g, lag)
                for kind, i, off in slots(lag):
                    if kind == "w":
                        if lag:
                            slab(A["w_branch"][g - 1, i], q, off)
                    else:
                        slab(A["w_in"][g, {"s": 0, "z": CT, "p": CT + GT}[kind] + i], q, off)

            slab(A["w_dt"], 0, 0)
            for c in range(4):
                sp.dma_start(ya[:, 4 * c:4 * c + 4, :], A["x"][:, 4 * c:4 * c + 4, :]).then_inc(x_in[c], 16)
            sp.dma_start(con, A["constants"]).then_inc(con_in, 16)
            sp.dma_start(par, A["params"]).then_inc(par_in, 16)
            sp.dma_start(scb, A["conv_rows"]).then_inc(scb_in, 16)
            iteration(0, False)
            with sp.Fori(1, G) as g:
                iteration(g, True)
            for i in range(GT):
                slab(A["w_branch"][G - 1, i], Q_TAIL, 2 + 2 * i)
            for i in range(4):
                slab(A["w_pool"][i], Q_POOL, 2 + 2 * i)
            with sp.Fori(0, KT // 2) as i:
                for j in range(4):
                    slab(A["w_gate"][4 * i + j], Q_GATE + 2 * i, 2 + 2 * j)
            with sp.Fori(0, KT // 4) as i:
                for j in range(4):
                    slab(A["w_out"][4 * i + j], Q_OUT + 2 * i, 2 + 2 * j)
            with sp.Fori(0, JF) as j:
                for w in range(2):
                    slab(A["w_up"][j, w], Q_UP + j, 2 + 2 * w)
            with sp.Fori(0, KT // 4) as i:
                for j in range(4):
                    at = 0
                    for n, tiles in enumerate(DOWN_TILES):
                        load(A["w_down"][4 * i + j, :, at * P:(at + tiles) * P], Q_DOWN + 6 * i, 2 + 6 * j + n, tiles)
                        at += tiles

        @block.gpsimd
        def _(pool):
            def load_state(g, i):
                slot, turn = i % 2, 2 * g + i // 2
                wait(pool, st_out[slot], 16 * turn)
                wait(pool, ty_ready, 4 * g + i - 1)
                pool.dma_start(st[:, slot].rearrange("p b t n -> p (b t n)"),
                               A["state"][g, i]).then_inc(st_in[slot], 16)

            def iteration(g, lag):
                wait(pool, conv_done, 24 * g)
                wait(pool, ust_done, g)
                pool.wait_ge(scb_in, 16)
                pool.tensor_copy(u_rows[:, :, :, 0:3], scb[:, g]).then_inc(ubuf_ready, 1)
                load_state(g, 0)
                load_state(g, 1)
                if not lag:
                    pool.wait_ge(con_in, 16)
                    pool.wait_ge(dt_dve, DT_TOK)
                for u in range(4):
                    wait(pool, bc_mm, 4 * g)
                    wait(pool, seg_mm, 4 * g + u)
                    pool.tensor_tensor(diag, tri.unsqueeze(1).to_broadcast([P, 4, P]),
                                       tok[:, 2 + u // 2, bass.ds(HG * g + 4 * (u % 2), 4)].unsqueeze(2)
                                       .to_broadcast([P, 4, P]), ALU.mult).then_inc(t_ready, 1)
                pool.wait_ge(acc_act, 12 * g + CT)
                pool.wait_ge(ubuf_ready, g + 1)
                pool.tensor_copy(cpo[:, g], u6[:, :, SEQ:SEQ + 3])
                pool.tensor_copy(scb[:, g], u_rows[:, :, :, 1:4]).then_inc(ust_done, 1)
                pool.wait_ge(xbc_ready, 2 * g + 1)
                for i in range(4):
                    wait(pool, seg_mm, 4 * g + 4)
                    wait(pool, bc_mm, 4 * g + i)
                    pool.tensor_tensor(diag, ident.unsqueeze(1).to_broadcast([P, 4, P]),
                                       xbc_s[:, i // 2, 4 * (i % 2):4 * (i % 2) + 4].unsqueeze(2)
                                       .to_broadcast([P, 4, P]), ALU.mult).then_inc(dg_ready, 1)
                pool.wait_ge(xbc_ready, 2 * g + 2)
                pool.wait_ge(exps_ready, 2 * g + 2)
                steps = 9 * g
                pool.tensor_tensor(dx, xbc_s[:, 2:CT].rearrange("p t b -> p b t"),
                                   exps[:, :, 0:NS].rearrange("p t b -> p b t"), ALU.mult).then_inc(pool_step, 1)
                pool.wait_ge(bc_ready, 4 * g + 4)
                pool.wait_ge(pool_step, steps + 1)
                for i in range(4):
                    slot = i % 2
                    pool.wait_ge(st_in[slot], 32 * g + 16 * (i // 2) + 16)
                    sv = st[:, slot]
                    da = exps[:, :, NS + 2 * i:NS + 2 * i + 2].rearrange("p t b -> p b t")
                    pool.tensor_tensor(sv, sv, da.unsqueeze(3).to_broadcast([P, 2, GT, P]),
                                       ALU.mult).then_inc(pool_step, 1)
                    rows_b = bc[:, i // 2, 2 * (i % 2):2 * (i % 2) + 2].unsqueeze(2).to_broadcast([P, 2, GT, P])
                    rows_c = bc[:, 2 + i // 2, 2 * (i % 2):2 * (i % 2) + 2].unsqueeze(2).to_broadcast([P, 2, GT, P])
                    wait(pool, snew, 4 * g + i)
                    pool.tensor_tensor(tm, rows_b, dx[:, 2 * i:2 * i + 2].unsqueeze(3).to_broadcast([P, 2, GT, P]),
                                       ALU.mult).then_inc(pool_step, 1)
                    if 1 <= i < 3:
                        load_state(g, i + 1)
                    pool.wait_ge(pool_step, steps + 1 + 2 * (i + 1))
                    pool.tensor_tensor(sv, sv, tm, ALU.add).then_inc(snew, 1)
                    wait(pool, red_done, 4 * g + i)
                    pool.wait_ge(snew, 4 * g + i + 1)
                    pool.tensor_tensor(ty, sv, rows_c, ALU.mult).then_inc(ty_ready, 1)
                    pool.dma_start(O["ssm_s"][g, i], sv.rearrange("p b t n -> p (b t n)")).then_inc(st_out[slot], 16)
                pool.wait_ge(st1_ready, g + 1)
                pool.dma_start(O["ssm_p"][g], s1).then_inc(s1_out, 16)

            iteration(0, False)
            with pool.Fori(1, G) as g:
                iteration(g, True)

            pool.wait_ge(s1_out, 16 * G)
            for slot in range(2):
                pool.wait_ge(st_out[slot], 32 * G)
            pool.wait_ge(red_done, 4 * G)
            pool.dma_start(spb, A["pool_rows"]).then_inc(spb_in, 16)
            pool.wait_ge(ust_done, G)
            pool.dma_start(O["conv_s"], scb).then_inc(conv_out, 16)
            pool.dma_start(O["conv_p"], cpo).then_inc(conv_out, 16)
            pool.memset(rsum, 0.0).then_inc(rsum_done, 1)
            pool.wait_ge(pool_rows, 2)
            pool.dma_start(O["pool_s"], spb).then_inc(pool_out, 16)
            pool.dma_start(O["pool_p"], ppo).then_inc(pool_out, 16)

            def sum_rows(base):
                with pool.Fori(0, KT) as m:
                    pool.wait_ge(res_ready, base + m + 1)
                    pool.wait_ge(rsum_done, base + base // KT + m + 1)
                    pool.tensor_tensor(rsum, rsum, res[:, m], ALU.add).then_inc(rsum_done, 1)

            sum_rows(0)
            pool.wait_ge(conv_out, 32)
            pool.wait_ge(pool_out, 32)
            pool.wait_ge(mean_mm, 1)
            pool.memset(rsum, 0.0).then_inc(rsum_done, 1)
            pool.memset(fpo, 0.0).then_inc(fst_done, 1)
            pool.dma_start(sfb, A["ffn_rows"]).then_inc(sfb_in, 16)
            pool.wait_ge(sfb_in, 16)
            uf_rows = uf[:, :, FFN_K - 1 + SEQ:FW].rearrange("p w (b f) -> p w b f", f=FFN_K)
            with pool.Fori(0, JF) as j:
                pool.wait_ge(fconv, 6 * j + 1)
                pool.wait_ge(fst_done, j + 1)
                pool.wait_ge(sfb_in, 16)
                pool.tensor_copy(uf_rows[:, :, :, 0:2], sfb[:, j]).then_inc(fbuf_ready, 1)
                pool.wait_ge(acc_act, ACT_UP + 2 * j + 2)
                pool.wait_ge(fbuf_ready, j + 1)
                pool.tensor_copy(fpo[:, j], uf[:, :, SEQ:SEQ + 2])
                pool.tensor_copy(sfb[:, j], uf_rows[:, :, :, 1:3]).then_inc(fst_done, 1)
            pool.wait_ge(fst_done, JF + 1)
            pool.dma_start(O["ffn_s"], sfb).then_inc(stored, 16)
            pool.dma_start(O["ffn_p"], fpo).then_inc(stored, 16)
            sum_rows(KT)
            pool.wait_ge(ln_ready, 2 * KT)
            pool.dma_start(O["y"], res).then_inc(stored, 16)
            pool.wait_ge(stored, 3 * 16)

        @block.tensor
        def _(pe):
            def half(q, off, tiles, hi, lo, bank_wait=None):
                slot = off % RING
                pe.wait_ge(lo_ready, 4 * q + off + 1)
                for n, (bank, k, first, last) in enumerate(tiles):
                    if first and bank_wait is not None:
                        bank_wait(n)
                    out = acc[bank][:, 0:T]
                    w_hi, w_lo = (w[:, slot, n * P:(n + 1) * P] for w in (whi, wlo))
                    pe.matmul(out, w_hi, hi[:, k], start=first, stop=False)
                    pe.matmul(out, w_hi, lo[:, k], start=False, stop=False)
                    ins = pe.matmul(out, w_lo, hi[:, k], start=False, stop=last)
                ins.then_inc(half_used, 1)

            def slab(q, off, bank, hi, lo, bank_wait):
                half(q, off, [(bank, k, k == 0, False) for k in range(HT)], hi, lo, bank_wait)
                half(q, off + 1, [(bank, HT + k, False, k == HT - 1) for k in range(HT)], hi, lo)

            def slab_of_4(q, off, banks, hi, lo, bank_wait):
                for h in range(2):
                    half(q, off + h, [(banks[2 * h + n // 4], n % 4, n % 4 == 0, n % 4 == 3) for n in range(HT)],
                         hi, lo, lambda n, h=h: bank_wait(2 * h + n // 4))

            def branch(q, off, i, before, first_wait):
                def bank_wait(r):
                    if i == 0:
                        first_wait(r)
                    else:
                        pe.wait_ge(acc_dve, before + 4 * (i - 1) + r + 1)
                return bank_wait

            for c in range(4):
                pe.wait_ge(xlo_ready, c + 1)
                if c % 2 == 0:
                    pe.wait_ge(lo_ready, c // 2 + 1)
                for k in range(4 * c, 4 * c + 4):
                    w_hi, w_lo = (w[:, k // HT, (k % HT) * P:(k % HT + 1) * P] for w in (whi, wlo))
                    pe.matmul(misc[:, 0:T], w_hi, xhi[:, k], start=k == 0, stop=False)
                    pe.matmul(misc[:, 0:T], w_hi, xlo[:, k], start=False, stop=False)
                    ins = pe.matmul(misc[:, 0:T], w_lo, xhi[:, k], start=False, stop=k == KT - 1)
                if c % 2 == 1:
                    ins.then_inc(half_used, 1)

            def dt_products():
                pe.wait_ge(con_in, 16)
                pe.wait_ge(dt_dve, DT_DONE)
                for n, row in enumerate((0, 0, 1, 1)):
                    ins = pe.transpose(seg_b[:, 64 * n:64 * n + 64], dts[0:64, row, P * (n % 2):P * (n % 2 + 1)],
                                       ident[0:64, 0:64])
                ins.then_inc(dt_mm, 1)
                pe.wait_ge(dt_dve, DT_TOK)
                da = tok[:, 2:4, :].rearrange("p c h -> p (c h)")
                pe.matmul(tp_b[:, 0:P], tri, da, start=True, stop=True)
                pe.matmul(tp_b[:, P:2 * P], ones, da, start=True, stop=True)
                pe.matmul(yd_b[0:64, 0:P], tok[:, 3, :], tri, start=True, stop=True).then_inc(dt_mm, 1)

            def per_channel(g):
                pe.wait_ge(exr_ready, g + 1)
                wait(pe, yo_read, g)
                wait(pe, ms_ready, g)
                for t in range(GT):
                    bank = (tp_b, misc)[t // 2]
                    ins = pe.matmul(bank[:, EW * (t % 2):EW * (t % 2 + 1)], con[:, K_E + P * t:K_E + P * (t + 1)],
                                    exg, start=True, stop=True)
                ins.then_inc(exp_mm, 1)

            def square_sum(turn):
                pe.wait_ge(vsq_ready, turn)
                pe.wait_ge(st1_ready, turn)
                pe.matmul(misc[:, 0:T], ones, rs[:, 1], start=True, stop=True).then_inc(ssq_mm, 1)

            def decay(g, u):
                pe.wait_ge(t_ready, 4 * g + u + 1)
                wait(pe, dec_ready, 4 * g + u)
                if u == 0:
                    wait(pe, yd_read, 8 * g)
                pe.matmul(seg_b[:, :], low, diag_f, start=True, stop=True).then_inc(seg_mm, 1)

            def rows(g, i):
                pe.wait_ge(dg_ready, 4 * g + i + 1)
                wait(pe, bc_ready, 4 * g + i)
                if i == 0:
                    wait(pe, yd_read, 8 * g)
                pe.matmul(yd_b[:, :], ones, diag_f, start=True, stop=True).then_inc(bc_mm, 1)

            def cb(g):
                pe.wait_ge(xbc_ready, 2 * g + 1)
                pe.wait_ge(exps_ready, 2 * g + 2)
                wait(pe, ms_ready, g)
                for c in range(2):
                    part = slice(c * P, (c + 1) * P)
                    pe.matmul(misc[:, part], xbc[:, 0, part], xbc[:, 1, part], start=True, stop=True)
                for c in range(2):
                    ins = pe.transpose(misc[:, (2 + c) * P:(3 + c) * P], xbc[:, 0, c * P:(c + 1) * P], ident)
                ins.then_inc(cb_mm, 1)

            def x_turned(g, c):
                pe.wait_ge(xbc_ready, 2 * g + 2)
                pe.wait_ge(exps_ready, 2 * g + 2)
                if c:
                    pe.wait_ge(xdt_ready, 4 * g + 2)
                for t in range(GT):
                    ins = pe.transpose(tp_b[:, t * P:(t + 1) * P], xbc[:, 2 + t, c * P:(c + 1) * P], ident)
                ins.then_inc(xt_mm, 1)

            def state(g, c):
                pe.wait_ge(xdt_ready, 4 * g + 2 * c + 2)
                pe.wait_ge(btok_ready, g + 1)
                pe.wait_ge(cbm_ready, g + 1)
                if c:
                    pe.wait_ge(s0_ready, g + 1)
                pe.matmul(misc[:, :], btok[:, c], xde[:, c], start=True, stop=True).then_inc(st_mm, 1)

            def y_heads(g, c):
                pe.wait_ge(m_ready, 4 * g + 2 * c + 2)
                pe.wait_ge(xdt_ready, 4 * g + 2 * c + 2)
                pe.wait_ge(bc_ready, 4 * g + 4)
                if c:
                    pe.wait_ge(yd_read, 8 * g + 4)
                for t in range(GT):
                    bank = (yd_b, seg_b)[t // 2]
                    ins = pe.matmul(bank[:, 256 * (t % 2):256 * (t % 2 + 1)], xdt[:, c, t * P:(t + 1) * P],
                                    dec[:, 2 * c + t // 2, 2 * (t % 2):2 * (t % 2) + 2].rearrange("p h i -> p (h i)"),
                                    start=True, stop=True)
                ins.then_inc(yd_mm, 1)

            def y_state(g):
                pe.wait_ge(s0_ready, g + 1)
                pe.wait_ge(xdt_ready, 4 * g + 4)
                for t in range(GT):
                    ins = pe.matmul(tp_b[:, t * P:(t + 1) * P], s0[:, t * P:(t + 1) * P], xbc[:, 1, P:2 * P],
                                    start=True, stop=True)
                ins.then_inc(yo_mm, 1)

            def iteration(g, lag):
                q = q_of(g, lag)
                seen = 0
                for kind, i, off in slots(lag):
                    if kind == "w":
                        if lag:
                            if i == 0:
                                pe.wait_ge(ylo_ready, g)
                            slab_of_4(q, off, [(2 + r) % 4 for r in range(4)], yhi, ylo,
                                      branch(q, off, i, GT * GT * (g - 1),
                                             lambda r: pe.wait_ge(acc_act, 12 * g + 3 + r)))
                    else:
                        if kind == "z" and lag:
                            free = (acc_dve, GT * GT * (g - 1) + 13 + i)
                        else:
                            free = (acc_act, 12 * g - 3 + seen)
                        slab(q, off, seen % 4, xhi, xlo, lambda n: wait(pe, *free))
                        seen += 1
                    if kind == "s":
                        if i == 2 and lag:
                            square_sum(g)
                        elif i == 4:
                            per_channel(g)
                        if i >= 2:
                            decay(g, i - 2)
                    elif kind == "w":
                        rows(g, i)
                        if i == 1:
                            cb(g)
                        elif i >= 2:
                            x_turned(g, i - 2)
                    elif kind == "z":
                        if i == 0:
                            state(g, 0)
                        elif i == 1:
                            y_heads(g, 0)
                        elif i == 2:
                            state(g, 1)
                            y_heads(g, 1)
                        else:
                            y_state(g)

            dt_products()
            pe.wait_ge(dt_act, DT_ACT)
            iteration(0, False)
            with pe.Fori(1, G) as g:
                iteration(g, True)

            square_sum(G)
            pe.wait_ge(ylo_ready, G)
            for i in range(GT):
                slab_of_4(Q_TAIL, 2 + 2 * i, range(4), yhi, ylo,
                          branch(None, None, i, GT * GT * (G - 1), lambda r: pe.wait_ge(acc_act, 12 * G - 3 + r)))
            for i in range(4):
                pe.wait_ge(plo_ready, i + 1)
                slab_of_4(Q_POOL, 2 + 2 * i, range(4), phi[:, i % 2], plo[:, i % 2],
                          (lambda r: pe.wait_ge(acc_dve, DVE_OUT - 3 + r)) if i == 0 else
                          (lambda r, i=i: pe.wait_ge(acc_act, ACT_POOL + 4 * i - 3 + r)))
            with pe.Fori(0, KT // 2) as i:
                for j in range(4):
                    slab(Q_GATE + 2 * i, 2 + 2 * j, j, xhi, xlo,
                         lambda n, j=j: pe.wait_ge(acc_act, ACT_GATE + 4 * i + j - 3))
            pe.wait_ge(acc_act, ACT_UP)
            pe.wait_ge(mlo_ready, KT)
            with pe.Fori(0, KT // 4) as i:
                for j in range(4):
                    slab(Q_OUT + 2 * i, 2 + 2 * j, j, mhi, mlo,
                         lambda n, j=j: pe.wait_ge(acc_dve, DVE_OUT + 4 * i + j - 3))

            def layer_norm(n):
                pe.wait_ge(rsum_done, (n + 1) * (KT + 1))
                pe.matmul(seg_b[:, 0:T], ones, rsum, start=True, stop=True).then_inc(mean_mm, 1)
                for c in range(4):
                    pe.wait_ge(sq_ready, 4 * n + c + 1)
                    for t in range(4):
                        ins = pe.matmul(tp_b[:, 0:T], ones, lsq[:, c % 2, t], start=c + t == 0, stop=c + t == 6)
                    ins.then_inc(sq_mm, 1)

            layer_norm(0)
            pe.wait_ge(x1lo_ready, 4)
            with pe.Fori(0, JF) as j:
                for w in range(2):
                    slab(Q_UP + j, 2 + 2 * w, w, x1hi, x1lo, lambda n, w=w: pe.wait_ge(acc_act, ACT_UP + 2 * j + w - 1))
            pe.wait_ge(acc_act, ACT_UP + 2 * JF)
            with pe.Fori(0, KT // 4) as i:
                for j in range(4):
                    k = 0
                    for n, tiles in enumerate(DOWN_TILES):
                        if j == 0 and n in (0, 5):
                            pe.wait_ge(flo_ready, JF if n else JF - 1)
                        half(Q_DOWN + 6 * i, 2 + 6 * j + n,
                             [(j, k + r, k + r == 0, k + r == JF - 1) for r in range(tiles)], hhi, hlo,
                             lambda n, j=j: pe.wait_ge(acc_dve, DVE_DOWN + 4 * i + j - 3))
                        k += tiles
            layer_norm(1)

        @block.scalar
        def _(act):
            def split(q, off, tiles=HT):
                slot = off % RING
                act.wait_ge(raw_landed[slot], 16 * (q + off // RING + 1))
                wait(act, half_used, 4 * q + off - RING + 1)
                part = slice(0, tiles * P)
                act.activation(whi[:, slot, part], raw[:, slot, part], ACT.Copy).then_inc(hi_ready, 1)

            def slab_done(q, off):
                split(q, off + RING)
                act.wait_ge(half_used, 4 * q + off + 2)

            split(0, 0)
            split(0, 1)
            for c in range(4):
                part = slice(4 * c, 4 * c + 4)
                act.wait_ge(x_in[c], 16)
                act.activation(xhi[:, part], ya[:, part], ACT.Copy).then_inc(xhi_ready, 1)
            for n in range(2, 6):
                split(0, n)

            act.wait_ge(par_in, 16)
            act.wait_ge(dt_dve, 4)
            act.activation(dts[0:64, 4], dts[0:64, 3], ACT.Exp, scale=-1.0).then_inc(dt_act, 1)
            act.activation(hcol[0:64, 0:1], par[0:64, C_HEAD + 1:C_HEAD + 2], ACT.Exp).then_inc(dt_act, 1)
            act.wait_ge(dt_dve, DT_DONE)
            act.activation(exr[0:64, NS:2 * NS], dts[0:64, 1, SEQ:T], ACT.Exp).then_inc(dt_act, 1)
            act.wait_ge(dt_mm, 2)
            act.activation(exr[0:64, 2 * NS + 2:EW], yd_b[0:64, 0:P], ACT.Exp).then_inc(dt_act, 1)
            act.wait_ge(dt_dve, DT_TOK + 2)
            act.activation(ctot.rearrange("p c h -> p (c h)"), tp_b[:, P:2 * P], ACT.Exp).then_inc(dt_act, 1)
            act.activation(fe.rearrange("p c h -> p (c h)"), fe.rearrange("p c h -> p (c h)"), ACT.Exp).then_inc(dt_act, 1)

            def iteration(g, lag):
                q = q_of(g, lag)
                seen = 0
                for kind, i, off in slots(lag):
                    if off is not None:
                        slab_done(q, off)
                    if kind == "s":
                        bank = acc[seen % 4]
                        if i == 0:
                            wait(act, conv_done, 24 * g)
                            wait(act, ust_done, g)
                        act.activation(u6[:, i, CONV_K - 1:CONV_K - 1 + SEQ], bank[:, 0:SEQ], ACT.Copy)
                        act.activation(u_rows[:, i, :, CONV_K - 1], bank[:, SEQ:T], ACT.Copy).then_inc(acc_act, 1)
                        seen += 1
                        split(q, off + RING + 1)
                        if i == 4:
                            act.wait_ge(exp_mm, g + 1)
                            wait(act, ty_ready, 4 * g)
                            wait(act, vsq_ready, g)
                            for h, part in enumerate((tp_b, misc)):
                                act.activation(exps[:, 2 * h:2 * h + 2], part[:, 0:2 * EW].rearrange(
                                    "p (t e) -> p t e", t=2), ACT.Copy).then_inc(exps_ready, 1)
                        if i == 3 and lag:
                            act.wait_ge(ms_ready, g)
                            act.activation(rs[:, 1], rs[:, 0], ACT.Sqrt).then_inc(std_ready, 1)
                        if i >= 2:
                            u = i - 2
                            act.wait_ge(seg_mm, 4 * g + u + 1)
                            act.activation(dec[:, u].rearrange("p h i -> p (h i)"), seg_b[:, :],
                                           ACT.Exp).then_inc(dec_ready, 1)
                        if i == 4 and lag:
                            act.wait_ge(y3_ready, 4 * g)
                            act.activation(yhi, y3, ACT.Copy).then_inc(yhi_ready, 1)
                        if i == 5:
                            for part, steps in ((slice(0, 2), 8), (slice(2, CT), 24)):
                                act.wait_ge(conv_done, 24 * g + steps)
                                act.activation(xbc[:, part], xbc[:, part], ACT.Silu).then_inc(xbc_ready, 1)
                    elif kind == "w":
                        if lag:
                            split(q, off + RING + 1)
                        act.wait_ge(bc_mm, 4 * g + i + 1)
                        wait(act, ty_ready, 4 * g)
                        act.activation(bc_f[:, i], yd_b[:, :], ACT.Copy).then_inc(bc_ready, 1)
                        if i == 1:
                            act.wait_ge(cb_mm, g + 1)
                            act.wait_ge(cbm_ready, g + 1)
                            act.activation(btok.rearrange("p c n -> p (c n)"), misc[:, 2 * P:4 * P],
                                           ACT.Copy).then_inc(btok_ready, 1)
                    elif kind == "z":
                        wait(act, vsq_ready, g)
                        act.activation(zs[:, i], acc[seen % 4][:, 0:T], ACT.Silu).then_inc(acc_act, 1)
                        seen += 1
                        split(q, off + RING + 1)
                        if i == 0:
                            act.wait_ge(st_mm, 2 * g + 1)
                            wait(act, st1_ready, g)
                            act.activation(s0, misc[:, :], ACT.Copy).then_inc(s0_ready, 1)
                        elif i < 3:
                            c = i - 1
                            act.wait_ge(yd_mm, 2 * g + i)
                            wait(act, y3_ready, 4 * g)
                            for b, bank in enumerate((yd_b, seg_b)):
                                for h in range(2):
                                    rows = slice(64 * h, 64 * h + 64)
                                    act.activation(yt[rows, 2 * b:2 * b + 2, c * P:(c + 1) * P],
                                                   bank[rows, :].rearrange("p (t h i) -> p t h i", t=2, h=2)[:, :, h],
                                                   ACT.Copy).then_inc(yd_read, 1)
                    else:
                        act.activation(poolu[:, 2 * g + i, 16:PW], acc[seen % 4][:, 0:T], ACT.Copy).then_inc(acc_act, 1)
                        seen += 1
                        split(q, off + RING + 1)

            iteration(0, False)
            with act.Fori(1, G) as g:
                iteration(g, True)

            act.wait_ge(ms_ready, G)
            act.activation(rs[:, 1], rs[:, 0], ACT.Sqrt).then_inc(std_ready, 1)
            act.wait_ge(y3_ready, 4 * G)
            act.activation(yhi, y3, ACT.Copy).then_inc(yhi_ready, 1)

            def round_pooled(i):
                act.wait_ge(pooled, i + 1)
                wait(act, half_used, 4 * Q_POOL + 2 + 2 * (i - 1))
                act.activation(phi[:, i % 2], pp, ACT.Copy).then_inc(phi_ready, 1)

            for i in range(GT):
                for h in range(2):
                    split(Q_TAIL, 2 + 2 * i + h + RING)
                if i % 2:
                    round_pooled(i // 2)
            for i in range(4):
                for h in range(2):
                    split(Q_POOL, 2 + 2 * i + h + RING)
                    act.wait_ge(half_used, 4 * Q_POOL + 3 + 2 * i + h)
                    for r in range(2 * h, 2 * h + 2):
                        m = 4 * i + r
                        act.activation(yb[:, m], acc[r][:, 0:T], ACT.Copy,
                                       scale=par[:, C_PSC + m:C_PSC + m + 1]).then_inc(acc_act, 1)
                if i < 2:
                    round_pooled(i + 2)
            act.wait_ge(conv_out, 32)
            with act.Fori(0, KT // 2) as i:
                for j in range(4):
                    slab_done(Q_GATE + 2 * i, 2 + 2 * j)
                    act.wait_ge(mx_step, 4 * i + 2 * (j // 2) + 1)
                    act.activation(sg[:, j], acc[j][:, 0:T], ACT.Sigmoid,
                                   bias=par[:, bass.ds(C_GATE + 4 * i + j, 1)]).then_inc(acc_act, 1)
                    split(Q_GATE + 2 * i, 2 + 2 * j + RING + 1)
                    if j % 2:
                        act.wait_ge(mx_ready, 2 * i + j // 2 + 1)
                        act.activation(mhi[:, 2 * i + j // 2], mx[:, j // 2, 0], ACT.Copy).then_inc(mhi_ready, 1)
            with act.Fori(0, KT // 4) as i:
                for n in range(8):
                    split(Q_OUT + 2 * i, 2 + n + RING)

            def layer_norm(n):
                for c in range(4):
                    act.wait_ge(rc_ready, 4 * n + c + 1)
                    wait(act, sq_mm, 4 * n + c - 1)
                    act.activation(lsq[:, c % 2], res[:, 4 * c:4 * c + 4], ACT.Square).then_inc(sq_ready, 1)
                act.wait_ge(var_ready, n + 1)
                act.activation(lnr[:, 2], lnr[:, 1], ACT.Sqrt).then_inc(lnstd, 1)

            layer_norm(0)
            act.wait_ge(pool_out, 32)
            for c in range(4):
                part = slice(4 * c, 4 * c + 4)
                act.wait_ge(ln_ready, 4 * c + 4)
                act.activation(x1hi[:, part], res[:, part], ACT.Copy).then_inc(x1hi_ready, 1)

            def gated_high(j):
                act.wait_ge(fh_ready, 2 * j + 2)
                act.activation(hhi[:, j], hh, ACT.Copy).then_inc(fhi_ready, 1)

            def up(j, first):
                for w in range(2):
                    q, off = Q_UP + j, 2 + 2 * w
                    split(q, off + RING)
                    if w:
                        act.wait_ge(fconv, 6 * j + 4)
                        act.activation(fc[:, 0], fc[:, 0], ACT.Silu).then_inc(fsilu, 1)
                    act.wait_ge(half_used, 4 * q + off + 2)
                    wait(act, fconv, 6 * j - 2 + 3 * w)
                    act.wait_ge(fst_done, j + 1)
                    act.activation(uf[:, w, FFN_K - 1:FFN_K - 1 + SEQ], acc[w][:, 0:SEQ], ACT.Copy)
                    act.activation(uf[:, w, FFN_K - 1 + SEQ:FW].rearrange("p (b f) -> p b f", f=FFN_K)[:, :, FFN_K - 1],
                                   acc[w][:, SEQ:T], ACT.Copy).then_inc(acc_act, 1)
                    split(q, off + RING + 1)
                    if not first and not w:
                        gated_high(j - 1)

            up(0, True)
            with act.Fori(1, JF) as j:
                up(j, False)
            gated_high(JF - 1)

            def down(i, last):
                for j in range(4):
                    for n in range(6):
                        if not (last and j == 3 and n >= 2):
                            split(Q_DOWN + 6 * i, 2 + 6 * j + n + RING, DOWN_TILES[(n + RING) % 6])

            with act.Fori(0, KT // 4 - 1) as i:
                down(i, False)
            down(KT // 4 - 1, True)
            layer_norm(1)

        @block.vector
        def _(dve):
            def split(q, off, tiles=HT):
                slot = off % RING
                dve.wait_ge(hi_ready, 4 * q + off + 1)
                part = slice(0, tiles * P)
                dve.tensor_tensor(wlo[:, slot, part], raw[:, slot, part], whi[:, slot, part].bitcast(F32),
                                  ALU.subtract).then_inc(lo_ready, 1)

            def head(row):
                return dts[0:64, row]

            chain = [0]

            def then(ins):
                ins.then_inc(dt_dve, 1)
                chain[0] += 1
                dve.wait_ge(dt_dve, chain[0])

            dve.memset(poolu[:, :, 0:16], 0.0)
            dve.memset(u6[:, :, 0:CONV_K - 1], 0.0).then_inc(zeroed, 1)
            split(0, 0)
            split(0, 1)
            for c in range(4):
                part = slice(4 * c, 4 * c + 4)
                dve.wait_ge(xhi_ready, c + 1)
                dve.tensor_tensor(xlo[:, part], ya[:, part], xhi[:, part].bitcast(F32),
                                  ALU.subtract).then_inc(xlo_ready, 1)
            for n in range(2, 6):
                split(0, n)
            dve.wait_ge(xlo_ready, 4)
            dve.memset(ya, 0.0).then_inc(zeroed, 1)
            then(dve.memset(exr, 0.0))
            dve.wait_ge(half_used, 2)
            dve.wait_ge(par_in, 16)
            then(dve.tensor_scalar(head(2), misc[0:64, 0:T], par[0:64, C_HEAD:C_HEAD + 1], None, ALU.add))
            then(dve.tensor_scalar(head(1), head(2), 0.0, None, ALU.max))
            then(dve.scalar_tensor_tensor(out=head(3), in0=head(1), scalar=2.0, in1=head(2),
                                          op0=ALU.mult, op1=ALU.subtract))
            dve.wait_ge(dt_act, 1)
            then(dve.tensor_scalar(head(5), head(4), 2.0, None, ALU.add))
            then(dve.reciprocal(head(6), head(5)))
            then(dve.tensor_tensor(head(3), head(4), head(6), ALU.mult))
            then(dve.tensor_tensor(head(4), head(3), head(3), ALU.mult))
            then(dve.tensor_scalar(head(5), head(4), 1.0 / 17, None, ALU.mult))
            for k in range(7, 0, -1):
                then(dve.scalar_tensor_tensor(out=head(5), in0=head(5), scalar=1.0 / (2 * k + 1), in1=head(4),
                                              op0=ALU.add, op1=ALU.mult))
            then(dve.scalar_tensor_tensor(out=head(5), in0=head(5), scalar=1.0, in1=head(3),
                                          op0=ALU.add, op1=ALU.mult))
            then(dve.scalar_tensor_tensor(out=head(0), in0=head(5), scalar=2.0, in1=head(1),
                                          op0=ALU.mult, op1=ALU.add))
            dve.wait_ge(dt_act, 2)
            then(dve.tensor_scalar(hcol[0:64, 1:2], hcol[0:64, 0:1], -1.0, None, ALU.mult))
            then(dve.tensor_scalar(head(1), head(0), hcol[0:64, 1:2], None, ALU.mult))
            assert chain[0] == DT_DONE
            dve.wait_ge(dt_mm, 1)
            then(dve.tensor_copy(tok.rearrange("p r h -> p (r h)"), seg_b[:, 0:4 * N_HEADS]))
            assert chain[0] == DT_TOK
            dve.wait_ge(dt_mm, 2)
            acs_f, fe_f = (x.rearrange("p c h -> p (c h)") for x in (acs, fe))
            then(dve.tensor_copy(acs_f, tp_b[:, 0:P]))
            then(dve.tensor_tensor(fe_f, tp_b[:, P:2 * P], acs_f, ALU.subtract))
            dve.wait_ge(dt_act, DT_ACT)
            then(dve.tensor_tensor(fe_f, fe_f, tok[:, 0:2].rearrange("p c h -> p (c h)"), ALU.mult))
            then(dve.tensor_copy(exr[0:64, 0:NS], dts[0:64, 0, SEQ:T]))
            then(dve.tensor_copy(exr[0:64, 2 * NS:2 * NS + 2],
                                 par[0:64, C_HEAD + 2:C_HEAD + 3].to_broadcast([64, 2])))

            state = {"n": 0, "base": 0}

            def step():
                state["n"] += 1
                return state["base"] + state["n"]

            def convolve(g, tiles, done):
                for k in range(CONV_K):
                    for s in tiles:
                        u, x = u6[:, s, k:k + CVW], xbc[:, s]
                        tap = conv_w[:, g, s, k:k + 1]
                        if k == 0:
                            ins = dve.tensor_scalar(x, u, tap, conv_w[:, g, s, CONV_K:CONV_K + 1], ALU.mult, ALU.add)
                        else:
                            dve.wait_ge(conv_done, 24 * g + done - 1)
                            ins = dve.scalar_tensor_tensor(out=x, in0=u, scalar=tap, in1=x, op0=ALU.mult, op1=ALU.add)
                        ins.then_inc(conv_done, 1)
                        done += 1

            def normalise(g, turn):
                dve.wait_ge(ssq_mm, turn)
                dve.tensor_scalar(rs[:, 0], misc[:, 0:T], 1.0 / (GT * P), EPS, ALU.mult, ALU.add).then_inc(ms_ready, 1)
                dve.wait_ge(std_ready, turn)
                dve.reciprocal(rs[:, 0], rs[:, 1]).then_inc(rstd_ready, 1)
                dve.wait_ge(rstd_ready, turn)
                for t in range(GT):
                    dve.scalar_tensor_tensor(out=y3[:, t], in0=yt[:, t], scalar=norm_w[:, g, t:t + 1], in1=rs[:, 0],
                                             op0=ALU.mult, op1=ALU.mult).then_inc(y3_ready, 1)

            def low_of_y(turn):
                dve.wait_ge(yhi_ready, turn)
                dve.tensor_tensor(ylo, y3, yhi.bitcast(F32), ALU.subtract).then_inc(ylo_ready, 1)

            def branch(q, off, i, first_bank):
                for h in range(2):
                    split(q, off + h + RING)
                    dve.wait_ge(half_used, 4 * q + off + h + 1)
                    for r in range(2 * h, 2 * h + 2):
                        m = 4 * i + r
                        dve.tensor_tensor(ya[:, m], ya[:, m], acc[(first_bank + r) % 4][:, 0:T],
                                          ALU.add).then_inc(acc_dve, 1)

            def sample_sum(g, i):
                dve.wait_ge(ty_ready, 4 * g + i + 1)
                dve.tensor_reduce(yt[:, :, SEQ + 2 * i:SEQ + 2 * i + 2].rearrange("p t b -> p b t"), ty, AX_X,
                                  ALU.add).then_inc(red_done, 1)

            def gate_y(turn):
                sample_sum(turn - 1, 3)
                dve.wait_ge(red_done, 4 * turn)
                dve.tensor_tensor(yt[:, :, SEQ:T], yt[:, :, SEQ:T], sml[:, 0], ALU.add).then_inc(dve_step, 1)
                now = step()
                dve.wait_ge(acc_act, 12 * turn)
                dve.wait_ge(dve_step, now)
                dve.tensor_tensor(yt, yt, zs, ALU.mult).then_inc(dve_step, 1)
                now = step()
                dve.wait_ge(dve_step, now)
                dve.tensor_tensor(y3, yt, yt, ALU.mult).then_inc(dve_step, 1)
                now = step()
                dve.wait_ge(dve_step, now)
                dve.tensor_reduce(rs[:, 1], y3.rearrange("p t i -> p i t"), AX_X, ALU.add).then_inc(vsq_ready, 1)

            def mask_decays(g, c, half):
                u = 2 * c + half
                dve.wait_ge(cbm_ready, g + 1)
                dve.wait_ge(dec_ready, 4 * g + u + 1)
                dve.tensor_tensor(dec[:, u], dec[:, u], cbm[:, c].unsqueeze(1).to_broadcast([P, 4, P]),
                                  ALU.mult).then_inc(m_ready, 1)

            def heads(row, g):
                return row[:, bass.ds(HG * g, HG)].unsqueeze(2).to_broadcast([P, HG, HEAD_DIM])

            def by_head(x):
                return x.rearrange("p (h d) -> p h d", h=HG)

            def iteration(g, lag):
                q = q_of(g, lag)
                wait(dve, exp_mm, g)
                if not lag:
                    dve.wait_ge(con_in, 16)
                    dve.wait_ge(zeroed, 2)
                dve.tensor_scalar(exg, exr, con[:, bass.ds(K_MASK + g, 1)], None, ALU.mult).then_inc(exr_ready, 1)
                for kind, i, off in slots(lag):
                    if kind == "w" and lag:
                        branch(q, off, i, 2)
                    elif off is not None:
                        split(q, off + RING)
                        if (kind, i) == ("s", CT - 1) and lag:
                            low_of_y(g)
                        split(q, off + RING + 1)
                    if kind == "s":
                        if lag:
                            if i == 1:
                                gate_y(g)
                            elif i == 3:
                                normalise(g - 1, g)
                        if i % 2:
                            if i == 1:
                                dve.wait_ge(ubuf_ready, g + 1)
                                wait(dve, yo_mm, g)
                                wait(dve, pool_step, 9 * g)
                                wait(dve, ty_ready, 4 * g)
                            dve.wait_ge(acc_act, 12 * g + i + 1)
                            convolve(g, (i - 1, i), 4 * (i - 1))
                    elif kind == "w":
                        if i == 1:
                            dve.wait_ge(cb_mm, g + 1)
                            dve.tensor_tensor(cbm, misc[:, 0:2 * P].rearrange("p (c i) -> p c i", c=2),
                                              tri.unsqueeze(1).to_broadcast([P, 2, P]), ALU.mult).then_inc(cbm_ready, 1)
                            dve.wait_ge(cbm_ready, g + 1)
                        elif i >= 2:
                            c = i - 2
                            dve.wait_ge(xt_mm, 2 * g + c + 1)
                            dve.tensor_tensor(by_head(xdt[:, c]), by_head(tp_b[:, :]), heads(tok[:, c], g),
                                              ALU.mult).then_inc(xdt_ready, 1)
                            dve.tensor_tensor(by_head(xde[:, c]), by_head(tp_b[:, :]), heads(fe[:, c], g),
                                              ALU.mult).then_inc(xdt_ready, 1)
                            mask_decays(g, 0, c)
                    elif kind == "z":
                        if i < 2:
                            mask_decays(g, 1, i)
                            sample_sum(g, i)
                        if i == 2:
                            wait(dve, s1_out, 16 * g)
                            dve.wait_ge(s0_ready, g + 1)
                            dve.tensor_tensor(by_head(s1), by_head(s0), heads(ctot[:, 1], g),
                                              ALU.mult).then_inc(dve_step, 1)
                            now = step()
                            dve.wait_ge(st_mm, 2 * g + 2)
                            dve.wait_ge(dve_step, now)
                            dve.tensor_tensor(s1, s1, misc[:, :], ALU.add).then_inc(st1_ready, 1)
                        if i == 3:
                            dve.wait_ge(yo_mm, g + 1)
                            part = y3[:, :, 0:P]
                            dve.tensor_tensor(part, tp_b[:, :].rearrange("p (t i) -> p t i", t=GT),
                                              exps[:, :, 2 * NS + 2:EW], ALU.mult).then_inc(yo_read, 1)
                            dve.wait_ge(yo_read, g + 1)
                            dve.wait_ge(yd_read, 8 * g + 8)
                            dve.tensor_tensor(yt[:, :, P:SEQ], yt[:, :, P:SEQ], part, ALU.add).then_inc(dve_step, 1)
                            now = step()
                            dve.wait_ge(dve_step, now)
                            for t in range(GT):
                                dve.scalar_tensor_tensor(out=yt[:, t, 0:SEQ], in0=xbc[:, 2 + t, 0:SEQ],
                                                         scalar=exps[:, t, 2 * NS:2 * NS + 1], in1=yt[:, t, 0:SEQ],
                                                         op0=ALU.mult, op1=ALU.add).then_inc(dve_step, 1)
                                step()
                            sample_sum(g, 2)
                            dve.tensor_tensor(sml[:, 0], xbc_s[:, 2:CT], exps[:, :, 2 * NS:2 * NS + 1].to_broadcast(
                                [P, GT, NS]), ALU.mult).then_inc(dve_step, 1)
                            step()

            iteration(0, False)
            first, state["n"] = state["n"], 0
            per_group = first + 3
            with dve.Fori(1, G) as g:
                state["base"] = per_group * g - 3
                iteration(g, True)
            assert state["n"] == per_group
            state["base"], state["n"] = per_group * G - 3, 0
            gate_y(G)
            normalise(G - 1, G)
            low_of_y(G)

            rc = con[:, K_RC:K_RC + 16]

            def pool_mix(i):
                win, part = WINDOWS[i], poolu[:, 4 * i:4 * i + 4]
                if i == 0:
                    dve.wait_ge(s1_out, 16 * G)
                    dve.wait_ge(st_out[0], 32 * G)
                    dve.wait_ge(st_out[1], 32 * G)
                src, width = part[:, :, 0:16 + SEQ], 1
                while width < win:
                    dst = pa if src is not pa else pb
                    lo = 2 * width - 1
                    dve.tensor_tensor(dst[:, :, lo:16 + SEQ], src[:, :, lo:16 + SEQ],
                                      src[:, :, lo - width:16 + SEQ - width], ALU.add).then_inc(dve_step, 1)
                    dve.wait_ge(dve_step, step())
                    src, width = dst, 2 * width
                if i:
                    dve.wait_ge(phi_ready, i)
                dve.scalar_tensor_tensor(out=pp[:, :, 0:SEQ], in0=src[:, :, 16:16 + SEQ], scalar=1.0 / win,
                                         in1=part[:, :, 16:16 + SEQ], op0=ALU.mult, op1=ALU.subtract
                                         ).then_inc(dve_step, 1)
                few = win - 1
                small = psm[:, :, 0:few]
                dve.tensor_tensor(small, src[:, :, 16:16 + few], rc[:, 0:few].unsqueeze(1).to_broadcast([P, 4, few]),
                                  ALU.mult).then_inc(dve_step, 1)
                step()
                dve.wait_ge(dve_step, step())
                dve.tensor_tensor(pp[:, :, 0:few], small, part[:, :, 16:16 + few], ALU.subtract).then_inc(dve_step, 1)
                step()
                if i == 0:
                    dve.wait_ge(spb_in, 16)
                    dve.tensor_copy(spb[:, :, :, POOL_BUF], poolu[:, :, 16 + SEQ:PW]).then_inc(pool_rows, 1)
                    dve.tensor_copy(ppo, poolu[:, :, 16 + SEQ - POOL_BUF:16 + SEQ]).then_inc(pool_rows, 1)
                    dve.wait_ge(pool_rows, 1)
                dve.tensor_reduce(psm[:, :, 16:16 + NS], spb[:, 4 * i:4 * i + 4, :, 16 - win:16], AX_X,
                                  ALU.add).then_inc(dve_step, 1)
                dve.wait_ge(dve_step, step())
                dve.scalar_tensor_tensor(out=pp[:, :, SEQ:T], in0=psm[:, :, 16:16 + NS], scalar=1.0 / win,
                                         in1=part[:, :, 16 + SEQ:PW], op0=ALU.mult, op1=ALU.subtract
                                         ).then_inc(pooled, 1)

            def low_of_pooled(i):
                dve.wait_ge(phi_ready, i + 1)
                dve.tensor_tensor(plo[:, i % 2], pp, phi[:, i % 2].bitcast(F32), ALU.subtract).then_inc(plo_ready, 1)

            for i in range(GT):
                branch(Q_TAIL, 2 + 2 * i, i, 0)
                if i % 2:
                    pool_mix(i // 2)
                    low_of_pooled(i // 2)
            for i in range(4):
                for h in range(2):
                    split(Q_POOL, 2 + 2 * i + h + RING)
                if i < 2:
                    pool_mix(i + 2)
                    low_of_pooled(i + 2)
            dve.memset(mx, 0.0).then_inc(mx_step, 1)
            with dve.Fori(0, KT // 2) as i:
                for j in range(4):
                    for h in range(2):
                        split(Q_GATE + 2 * i, 2 + 2 * j + h + RING)
                    if j % 2:
                        a = j // 2
                        m = 2 * i + a
                        dve.wait_ge(acc_act, ACT_GATE + 4 * i + j + 1)
                        dve.tensor_tensor(mx[:, a, 0], sg[:, j - 1], ya[:, m], ALU.mult).then_inc(mx_step, 1)
                        dve.tensor_tensor(mx[:, a, 1], sg[:, j], yb[:, m], ALU.mult).then_inc(mx_step, 1)
                        dve.wait_ge(mx_step, 4 * i + 2 * a + 3)
                        dve.tensor_tensor(mx[:, a, 0], mx[:, a, 0], mx[:, a, 1], ALU.add).then_inc(mx_ready, 1)
                        dve.wait_ge(mhi_ready, m + 1)
                        dve.tensor_tensor(mlo[:, m], mx[:, a, 0], mhi[:, m].bitcast(F32),
                                          ALU.subtract).then_inc(mlo_ready, 1)

            def residual(bank, m, hi, lo, count):
                dve.scalar_tensor_tensor(out=res[:, m], in0=hi[:, m].bitcast(F32), scalar=ALPHA, in1=acc[bank][:, 0:T],
                                         op0=ALU.mult, op1=ALU.add).then_inc(acc_dve, 1)
                dve.wait_ge(acc_dve, count)
                dve.scalar_tensor_tensor(out=res[:, m], in0=lo[:, m].bitcast(F32), scalar=ALPHA, in1=res[:, m],
                                         op0=ALU.mult, op1=ALU.add).then_inc(res_ready, 1)

            with dve.Fori(0, KT // 4) as i:
                for j in range(4):
                    split(Q_OUT + 2 * i, 2 + 2 * j + RING)
                    dve.wait_ge(half_used, 4 * (Q_OUT + 2 * i) + 4 + 2 * j)
                    residual(j, 4 * i + j, xhi, xlo, DVE_OUT + 4 * i + j + 1)
                    split(Q_OUT + 2 * i, 2 + 2 * j + RING + 1)

            def layer_norm(n):
                def wide(row):
                    return lnr[:, row].unsqueeze(1).to_broadcast([P, 4, T])

                dve.wait_ge(mean_mm, n + 1)
                dve.wait_ge(res_ready, KT * (n + 1))
                dve.tensor_scalar(lnr[:, 0], seg_b[:, 0:T], 1.0 / D_MODEL, None, ALU.mult).then_inc(mu_ready, 1)
                dve.wait_ge(mu_ready, n + 1)
                for c in range(4):
                    part = res[:, 4 * c:4 * c + 4]
                    dve.tensor_tensor(part, part, wide(0), ALU.subtract).then_inc(rc_ready, 1)
                dve.wait_ge(sq_mm, 4 * n + 4)
                dve.tensor_scalar(lnr[:, 1], tp_b[:, 0:T], 1.0 / D_MODEL, EPS, ALU.mult, ALU.add).then_inc(var_ready, 1)
                dve.wait_ge(lnstd, n + 1)
                dve.reciprocal(lnr[:, 3], lnr[:, 2]).then_inc(lnr_ready, 1)
                dve.wait_ge(lnr_ready, n + 1)
                for c in range(4):
                    part = res[:, 4 * c:4 * c + 4]
                    dve.tensor_tensor(part, part, wide(3), ALU.mult).then_inc(norm_step, 1)
                    dve.wait_ge(norm_step, 4 * n + c + 1)
                    for m in range(4 * c, 4 * c + 4):
                        g_col = C_LN + 2 * KT * n + m
                        dve.tensor_scalar(res[:, m], res[:, m], par[:, g_col:g_col + 1],
                                          par[:, g_col + KT:g_col + KT + 1], ALU.mult, ALU.add).then_inc(ln_ready, 1)
                    if n == 0 and c:
                        low_of_x1(c - 1)
                if n == 0:
                    low_of_x1(3)

            def low_of_x1(c):
                part = slice(4 * c, 4 * c + 4)
                dve.wait_ge(x1hi_ready, c + 1)
                dve.tensor_tensor(x1lo[:, part], res[:, part], x1hi[:, part].bitcast(F32),
                                  ALU.subtract).then_inc(x1lo_ready, 1)

            layer_norm(0)
            dve.memset(uf[:, :, 0:FFN_K - 1], 0.0).then_inc(fconv, 1)
            dve.wait_ge(fconv, 1)
            fc_s = fc[:, :, SEQ:FCW].rearrange("p w (b f) -> p w b f", f=FFN_K)

            def gated_product(j):
                dve.wait_ge(fsilu, j + 1)
                dve.wait_ge(fconv, 6 * j + 7)
                wait(dve, flo_ready, j)
                dve.tensor_tensor(hh[:, 0:SEQ], fc[:, 0, 0:SEQ], fc[:, 1, 0:SEQ], ALU.mult).then_inc(fh_ready, 1)
                dve.tensor_tensor(hh[:, SEQ:T], fc_s[:, 0, :, FFN_K - 1], fc_s[:, 1, :, FFN_K - 1],
                                  ALU.mult).then_inc(fh_ready, 1)

            def gated_low(j):
                dve.wait_ge(fhi_ready, j + 1)
                dve.tensor_tensor(hlo[:, j], hh, hhi[:, j].bitcast(F32), ALU.subtract).then_inc(flo_ready, 1)

            def up(j, first):
                for w in range(2):
                    split(Q_UP + j, 2 + 2 * w + RING)
                    if not first:
                        (gated_low if w else gated_product)(j - 1)
                    split(Q_UP + j, 2 + 2 * w + RING + 1)
                    dve.wait_ge(acc_act, ACT_UP + 2 * j + w + 1)
                    dve.wait_ge(fbuf_ready, j + 1)
                    wait(dve, fh_ready, 2 * j)
                    for k in range(FFN_K):
                        u, y = uf[:, w, k:k + FCW], fc[:, w]
                        if k == 0:
                            ins = dve.tensor_scalar(y, u, fc_w[:, j, w, 0:1], fc_w[:, j, w, FFN_K:FFN_K + 1],
                                                    ALU.mult, ALU.add)
                        else:
                            dve.wait_ge(fconv, 6 * j + 3 * w + k + 1)
                            ins = dve.scalar_tensor_tensor(out=y, in0=u, scalar=fc_w[:, j, w, k:k + 1], in1=y,
                                                           op0=ALU.mult, op1=ALU.add)
                        ins.then_inc(fconv, 1)

            up(0, True)
            with dve.Fori(1, JF) as j:
                up(j, False)
            gated_product(JF - 1)
            gated_low(JF - 1)

            def down(i, last):
                for j in range(4):
                    for n in range(6):
                        if not (last and j == 3 and n >= 2):
                            split(Q_DOWN + 6 * i, 2 + 6 * j + n + RING, DOWN_TILES[(n + RING) % 6])
                    dve.wait_ge(half_used, 4 * (Q_DOWN + 6 * i) + 2 + 6 * j + 6)
                    residual(j, 4 * i + j, x1hi, x1lo, DVE_DOWN + 4 * i + j + 1)

            with dve.Fori(0, KT // 4 - 1) as i:
                down(i, False)
            down(KT // 4 - 1, True)
            layer_norm(1)


def kernel(x_prompt, x_sample, state_ssm, state_ssd_conv, state_pool, state_ffn_conv, w_in, b_gate, conv_w, conv_b,
           dt_bias, a_log, d_skip, ssd_norm_w, w_ssd_branch, w_pool, pool_scale, w_out, ln1_g, ln1_b, w_up,
           ffn_conv_w, ffn_conv_b, w_down, ln2_g, ln2_b):
    import concourse.bacc as _bacc
    from concourse.bass_utils import run_bass_kernel_spmd as _run

    f32 = np.float32

    def arr(a):
        return np.asarray(a)

    def blocks(w, cols, k_tiles):
        w = w.reshape(k_tiles, P, -1)
        return np.stack([w[:, :, c:c + P].transpose(1, 0, 2).reshape(P, -1) for c in cols])

    def columns(v):
        return v.reshape(-1, P).T

    w_in, w_up, w_down = arr(w_in)[0], arr(w_up)[0], arr(w_down)[0]
    off_x, off_dt = D_INNER, 2 * D_INNER + 2 * G * D_STATE
    off_b = off_x + D_INNER
    off_pool, off_gate = off_dt + N_HEADS, off_dt + N_HEADS + D_MODEL
    group_cols = [[off_b + P * g, off_b + P * (G + g)] + [off_x + P * (GT * g + t) for t in range(GT)]
                  + [P * (GT * g + t) for t in range(GT)] + [off_pool + P * (2 * g + i) for i in range(2)]
                  for g in range(G)]
    conv_tiles = [[GT * G + g, GT * G + G + g] + [GT * g + t for t in range(GT)] for g in range(G)]
    x = np.concatenate([arr(x_prompt)[0], arr(x_sample)[:, 0]])

    cw = np.concatenate([arr(conv_w)[0], arr(conv_b)]).reshape(CONV_K + 1, -1, P)[:, conv_tiles]
    fcw = np.concatenate([arr(ffn_conv_w)[0], arr(ffn_conv_b)]).reshape(FFN_K + 1, 2, JF, P)
    heads = np.zeros((P, 3), f32)
    for i, v in enumerate((dt_bias, a_log, d_skip)):
        heads[:N_HEADS, i] = arr(v)[0]
    params = np.concatenate([
        cw.transpose(3, 1, 2, 0).reshape(P, -1), columns(arr(ssd_norm_w)[0]),
        arr(b_gate)[0].reshape(2, KT, P).transpose(2, 1, 0).reshape(P, -1), columns(arr(pool_scale)[0]),
        *(columns(arr(v)[0]) for v in (ln1_g, ln1_b, ln2_g, ln2_b)),
        fcw.transpose(3, 2, 1, 0).reshape(P, -1), heads], axis=1)

    r = np.arange(P)
    con = np.zeros((P, N_CON), f32)
    con[:, K_ID:K_ID + P] = r[:, None] == r[None, :]
    con[:, K_TRI:K_TRI + P] = r[:, None] <= r[None, :]
    con[:, K_LOW:K_LOW + P] = r[:, None] > r[None, :]
    con[:, K_ONE:K_ONE + P] = 1
    for t in range(GT):
        con[:N_HEADS, K_E + P * t:K_E + P * (t + 1)] = (r[:N_HEADS, None] % HG) == 2 * t + r[None, :] // HEAD_DIM
    con[:N_HEADS, K_MASK:K_MASK + G] = r[:N_HEADS, None] // HG == np.arange(G)
    con[:, K_RC:K_RC + 16] = f32(1) / np.arange(1, 17, dtype=f32)

    wb = arr(w_ssd_branch)[0].reshape(G, GT, P, 4, GT, P)
    wp = arr(w_pool)[0].reshape(4, 4, P, 4, P)
    st = arr(state_ssm)[0].reshape(4, 2, G, GT, P, D_STATE)
    arrays = {
        "x": x.reshape(T, KT, P).transpose(2, 1, 0),
        "w_dt": blocks(w_in, [off_dt], KT)[0],
        "w_in": np.stack([blocks(w_in, c, KT) for c in group_cols]),
        "w_branch": wb.transpose(0, 3, 2, 4, 1, 5).reshape(G, 4, P, -1),
        "w_pool": wp.transpose(0, 2, 3, 1, 4).reshape(4, P, -1),
        "w_gate": blocks(w_in, [off_gate + D_MODEL * h + P * m for m in range(KT) for h in range(2)], KT),
        "w_out": blocks(arr(w_out)[0], [P * m for m in range(KT)], KT),
        "w_up": blocks(w_up, [D_FF * h + P * j for j in range(JF) for h in range(2)], KT).reshape(JF, 2, P, -1),
        "w_down": blocks(w_down, [P * m for m in range(KT)], JF),
        "constants": con,
        "params": params,
        "state": st.transpose(2, 0, 4, 1, 3, 5).reshape(G, 4, P, -1),
        "conv_rows": arr(state_ssd_conv)[0].reshape(NS, 3, -1, P)[:, :, conv_tiles].transpose(4, 2, 3, 0, 1),
        "pool_rows": np.concatenate([arr(state_pool)[0], np.zeros((NS, 1, D_MODEL), f32)], axis=1)
        .reshape(NS, 16, KT, P).transpose(3, 2, 0, 1),
        "ffn_rows": arr(state_ffn_conv)[0].reshape(NS, 2, 2, JF, P).transpose(4, 3, 2, 0, 1),
    }
    outs = {
        "y": (P, KT, T), "ssm_p": (G, P, GT * P), "conv_p": (P, G, CT, 3), "pool_p": (P, KT, POOL_BUF),
        "ffn_p": (P, JF, 2, 2), "ssm_s": (G, 4, P, 2 * GT * P), "conv_s": (P, G, CT, NS, 3),
        "pool_s": (P, KT, NS, 16), "ffn_s": (P, JF, 2, NS, 2),
    }
    nc = _bacc.Bacc("TRN2", target_bir_lowering=False, num_devices=1, dynamic_dma_scratch_size=4096)
    arrays = {k: np.ascontiguousarray(v) for k, v in arrays.items()}
    A = {k: nc.dram_tensor(f"in_{k}", v.shape, F32, kind="ExternalInput").ap() for k, v in arrays.items()}
    O = {k: nc.dram_tensor(f"out_{k}", s, F32, kind="ExternalOutput").ap() for k, s in outs.items()}
    bass_hybrid_layer(nc, A, O)
    r = _run(nc, [{f"in_{k}": v for k, v in arrays.items()}], core_ids=[0]).results[0]
    r = {k: r[f"out_{k}"] for k in outs}

    y = r["y"].transpose(2, 1, 0).reshape(T, D_MODEL)

    def conv_rows(a):
        a = np.moveaxis(a, 0, -1)
        rows = a.shape[2:-1]
        parts = [a[:, 2:].reshape(G * GT, *rows, P), a[:, 0], a[:, 1]]
        a = np.concatenate(parts)
        return np.moveaxis(a, 0, -2).reshape(*rows, -1)

    return (
        y[:SEQ][None], y[SEQ:][:, None],
        r["ssm_p"].transpose(0, 2, 1).reshape(1, 1, N_HEADS, HEAD_DIM, D_STATE),
        conv_rows(r["conv_p"])[None, None],
        r["pool_p"].transpose(2, 1, 0).reshape(1, 1, POOL_BUF, D_MODEL),
        r["ffn_p"].transpose(3, 2, 1, 0).reshape(1, 1, 2, 2 * D_FF),
        r["ssm_s"].reshape(G, 4, P, 2, GT, D_STATE).transpose(1, 3, 0, 4, 2, 5)
        .reshape(1, NS, N_HEADS, HEAD_DIM, D_STATE),
        conv_rows(r["conv_s"])[None],
        r["pool_s"][:, :, :, 1:].transpose(2, 3, 1, 0).reshape(1, NS, POOL_BUF, D_MODEL),
        r["ffn_s"].transpose(3, 4, 2, 1, 0).reshape(1, NS, 2, 2 * D_FF),
    )
```

```python
from contextlib import ExitStack

import numpy as np

import concourse.bass as bass
from concourse import mybir

F32 = mybir.dt.float32
F32R = mybir.dt.float32r
ACT = mybir.ActivationFunctionType
ALU = mybir.AluOpType
AX_X = mybir.AxisListType.X

P = 128
D_MODEL = 2048
SEQ = 256
NS = 8
T = SEQ + NS
D_INNER = 2 * D_MODEL
HEAD_DIM = 64
N_HEADS = D_INNER // HEAD_DIM
G = 8
D_STATE = 128
CONV_K = 4
CHUNK = 128
WINDOWS = (2, 4, 8, 16)
POOL_BUF = max(WINDOWS) - 1
D_FF = 5504
FFN_K = 3
ALPHA = 2.0 ** 0.25
EPS = 1e-5

KT = D_MODEL // P
GT = D_INNER // G // P
HG = N_HEADS // G
JF = D_FF // P
CT = 2 + GT
UW = CONV_K - 1 + SEQ + NS * CONV_K
CVW = UW - (CONV_K - 1)
PW = 16 + T
FW = FFN_K - 1 + SEQ + NS * FFN_K
FCW = FW - (FFN_K - 1)
HT = 8
RING = 4
EW = 2 * NS + 2 + CHUNK

C_CONV = 0
C_NORM = C_CONV + G * CT * 5
C_GATE = C_NORM + G * GT
C_PSC = C_GATE + 2 * KT
C_LN = C_PSC + KT
C_FC = C_LN + 4 * KT
C_HEAD = C_FC + JF * 2 * 4
N_PAR = C_HEAD + 3
K_ID, K_TRI, K_LOW, K_ONE, K_E = 0, P, 2 * P, 3 * P, 4 * P
K_MASK = K_E + GT * P
K_RC = K_MASK + G
N_CON = K_RC + 16


def wait(e, sem, value):
    if not (isinstance(value, int) and value <= 0):
        e.wait_ge(sem, value)



def bass_hybrid_layer(nc, A, O):
    ctx = ExitStack()
    with ctx:
        def sem(name):
            return ctx.enter_context(nc.semaphore(name))

        place = [(nc.sbuf_base + 63) // 64 * 64]

        def sb(name, shape, dt=F32):
            offset = place[0]
            place[0] += (int(np.prod(shape)) * 4 + 31) // 32 * 32
            assert place[0] <= nc.sbuf_usable_end, (name, place[0], nc.sbuf_usable_end)
            return nc.alloc_sbuf_tensor_at(name, [P, *shape], dt, offset=offset).ap()

        raw = sb("w_raw", [RING, HT * P])
        whi = sb("w_hi", [RING, HT * P], F32R)
        wlo = sb("w_lo", [RING, HT * P], F32R)
        con = sb("constants", [N_CON])
        par = sb("params", [N_PAR])
        rsum = sb("row_sum", [T])
        ident, tri, low, ones = (con[:, k:k + P] for k in (K_ID, K_TRI, K_LOW, K_ONE))
        conv_w = par[:, C_CONV:C_NORM].rearrange("p (g s k) -> p g s k", g=G, s=CT)
        norm_w = par[:, C_NORM:C_GATE].rearrange("p (g t) -> p g t", g=G)
        fc_w = par[:, C_FC:C_HEAD].rearrange("p (j w k) -> p j w k", j=JF, w=2)

        arena = place[0]
        xhi = sb("x_hi", [KT, T], F32R)
        xlo = sb("x_lo", [KT, T], F32R)
        ya = sb("branch_a", [KT, T])
        poolu = sb("pool_in", [KT, PW])

        staging = place[0]
        u6 = sb("conv_in", [CT, UW])
        xbc = sb("xbc", [CT, CVW])
        scb_at = place[0]
        scb = sb("conv_rows_s", [G, CT, NS, 3])
        cpo = sb("conv_rows_p", [G, CT, 3])
        behind_rows = place[0]
        diag = sb("pe_right", [4, P])
        dec = sb("decay", [4, 4, P])
        cbm = sb("cb_masked", [2, P])
        btok = sb("b_tok", [2, P])
        xdt = sb("xdt", [2, GT * P])
        xde = sb("xdt_end", [2, GT * P])
        s0 = sb("state_0", [GT * P])
        s1 = sb("state_1", [GT * P])
        at_bc = place[0]
        bc = sb("bc_rows", [4, 4, P])
        st = sb("state_s", [2, 2, GT, P])
        tm = sb("state_add", [2, GT, P])
        ty = sb("state_c", [2, GT, P])
        exps = sb("per_channel", [GT, EW])
        exr = sb("per_head", [EW])
        exg = sb("per_head_group", [EW])
        dx = sb("dt_x", [NS, GT])
        zs = sb("z_silu", [GT, T])
        yt = sb("y", [GT, T])
        y3 = sb("y_normed", [GT, T])
        yhi = sb("y_hi", [GT, T], F32R)
        ylo = sb("y_lo", [GT, T], F32R)
        rs = sb("rstd", [2, T])
        tok = sb("per_token", [4, N_HEADS])
        acs = sb("a_cum", [2, N_HEADS])
        fe = sb("dt_end", [2, N_HEADS])
        ctot = sb("decay_total", [2, N_HEADS])
        hcol = sb("head_cols", [2])
        sml = sb("small_d", [2, GT, NS])
        place[0] = at_bc
        dts = sb("dt_steps", [7, T])

        place[0] = staging
        pa = sb("pool_a", [4, 16 + SEQ])
        pb = sb("pool_b", [4, 16 + SEQ])
        pp = sb("pooled", [4, T])
        assert place[0] <= scb_at
        place[0] = behind_rows
        phi = sb("pooled_hi", [2, 4, T], F32R)
        plo = [sb("pooled_lo_0", [4, T], F32R)]

        place[0] = staging
        mhi = sb("mix_hi", [KT, T], F32R)
        mlo = sb("mix_lo", [KT, T], F32R)
        sg = sb("gate_sig", [4, T])
        psm = sb("pool_small", [4, 16 + NS])
        plo.append(sb("pooled_lo_1", [4, T], F32R))
        spb = sb("pool_rows_s", [KT, NS, 16])
        ppo = sb("pool_rows_p", [KT, POOL_BUF])
        yb = sb("branch_b", [KT, T])
        qa = sb("pool_c", [4, 16 + SEQ])
        qb = sb("pool_d", [4, 16 + SEQ])
        mx = sb("mix_parts", [2, 2, T])

        place[0] = arena
        hhi = sb("h_hi", [JF, T], F32R)
        hlo = sb("h_lo", [JF, T], F32R)
        x1hi = sb("x1_hi", [KT, T], F32R)
        x1lo = sb("x1_lo", [KT, T], F32R)
        res = sb("residual", [KT, T])
        uf = sb("ffn_in", [2, FW])
        fc = sb("ffn_conv", [2, FCW])
        hh = sb("ffn_gated", [T])
        sfb = sb("ffn_rows_s", [JF, 2, NS, 2])
        fpo = sb("ffn_rows_p", [JF, 2, 2])
        lnr = sb("ln_rows", [4, T])
        lsq = sb("ln_squares", [2, 4, T])

        acc = [ctx.enter_context(nc.psum_tensor(f"acc{i}", [P, 512], F32)) for i in range(4)]
        seg_b, tp_b, yd_b, misc = (ctx.enter_context(nc.psum_tensor(n, [P, 512], F32))
                                   for n in ("seg", "turned", "y_heads", "misc"))

        raw_landed = [sem(f"raw_landed{i}") for i in range(RING)]
        hi_ready, lo_ready, half_used = sem("hi_ready"), sem("lo_ready"), sem("half_used")
        acc_act, acc_dve = sem("acc_act"), sem("acc_dve")
        con_in, par_in, scb_in, x_in = sem("con_in"), sem("par_in"), sem("scb_in"), [sem(f"x_in{i}") for i in range(4)]
        spb_in, sfb_in = sem("spb_in"), sem("sfb_in")
        st_in, st_out = [sem(f"st_in{i}") for i in range(2)], [sem(f"st_out{i}") for i in range(2)]
        xhi_ready, xlo_ready, zeroed, ya_zeroed = sem("xhi_ready"), sem("xlo_ready"), sem("zeroed"), sem("ya_zeroed")
        dt_act, dt_mm, dt_dve = sem("dt_act"), sem("dt_mm"), sem("dt_dve")
        exr_ready, exp_mm, exps_ready = sem("exr_ready"), sem("exp_mm"), sem("exps_ready")
        ubuf_ready, conv_done, ust_done = sem("ubuf_ready"), sem("conv_done"), sem("ust_done")
        xbc_ready = sem("xbc_ready")
        t_ready, seg_mm, dec_ready, m_ready = sem("t_ready"), sem("seg_mm"), sem("dec_ready"), sem("m_ready")
        dg_ready, bc_mm, bc_ready = sem("dg_ready"), sem("bc_mm"), sem("bc_ready")
        cb_mm, cbm_ready, btok_ready = sem("cb_mm"), sem("cbm_ready"), sem("btok_ready")
        xt_mm, xdt_ready = sem("xt_mm"), sem("xdt_ready")
        st_mm, s0_ready, st1_ready, s1_out = sem("st_mm"), sem("s0_ready"), sem("st1_ready"), sem("s1_out")
        yd_mm, yd_read, yo_mm, yo_read = sem("yd_mm"), sem("yd_read"), sem("yo_mm"), sem("yo_read")
        pool_step, snew, ty_ready, red_done = sem("pool_step"), sem("snew"), sem("ty_ready"), sem("red_done")
        dve_step = sem("dve_step")
        vsq_ready, ssq_mm, ms_ready, std_ready = sem("vsq_ready"), sem("ssq_mm"), sem("ms_ready"), sem("std_ready")
        rstd_ready, y3_ready, yhi_ready, ylo_ready = sem("rstd_ready"), sem("y3_ready"), sem("yhi_ready"), sem("ylo_ready")
        pooled, phi_ready, plo_ready, pool_rows = sem("pooled"), sem("phi_ready"), sem("plo_ready"), sem("pool_rows")
        widest_sum = sem("widest_sum")
        yb_ready, mx_step, mx_ready, mhi_ready, mlo_ready = (sem("yb_ready"), sem("mx_step"), sem("mx_ready"),
                                                             sem("mhi_ready"), sem("mlo_ready"))
        res_step, res_ready, rsum_done, mean_mm, mu_ready = (sem("res_step"), sem("res_ready"), sem("rsum_done"),
                                                             sem("mean_mm"), sem("mu_ready"))
        rc_ready, sq_ready, sq_mm, var_ready, lnstd, lnr_ready = (sem("rc_ready"), sem("sq_ready"), sem("sq_mm"),
                                                                  sem("var_ready"), sem("lnstd"), sem("lnr_ready"))
        even_normed, odd_normed, y_even, y_odd = (sem("even_normed"), sem("odd_normed"), sem("y_even"), sem("y_odd"))
        x1hi_ready, x1lo_even, x1lo_odd = sem("x1hi_ready"), sem("x1lo_even"), sem("x1lo_odd")
        fbuf_ready, fconv, fst_done, fsilu, fh_ready, fhi_ready, flo_ready = (
            sem("fbuf_ready"), sem("fconv"), sem("fst_done"), sem("fsilu"), sem("fh_ready"), sem("fhi_ready"),
            sem("flo_ready"))
        conv_out, pool_out, stored, y_stored = sem("conv_out"), sem("pool_out"), sem("stored"), sem("y_stored")

        FIRST_HALF = 2
        S_SLABS, W_SLABS, Z_SLABS = ([(kind, i) for i in range(n)] for kind, n in (("s", CT), ("w", GT), ("z", GT)))
        WITH_W = S_SLABS + W_SLABS + Z_SLABS + [("p", 0), ("p", 1)]
        WITHOUT_W = S_SLABS + [("p", 0)] + W_SLABS[:2] + [("p", 1)] + W_SLABS[2:] + Z_SLABS
        DT_DONE, DT_TOK, DT_ACT = 20, 21, 6
        ACT_POOL, ACT_GATE, ACT_UP = 12 * G + 4, 12 * G + KT, 12 * G + KT + 2 * KT
        DVE_OUT, DVE_DOWN = GT * GT * G, GT * GT * G + KT
        Q_EARLY, Q_TAIL, Q_POOL, Q_GATE, Q_OUT, Q_UP, Q_DOWN = 62, 64, 66, 66, 82, 90, 133
        DOWN_TILES = [8, 7, 7, 7, 7, 7]
        N_HALVES = 4 * (Q_DOWN + 24) + 2

        def q_of(g, lag):
            return 8 * g - 2 if lag else 0

        def slots(lag):
            off, out = FIRST_HALF, []
            for kind, i in WITH_W if lag else WITHOUT_W:
                if kind == "w" and not lag:
                    out.append((kind, i, None))
                else:
                    out.append((kind, i, off))
                    off += 2
            return out

        def prompt_and_rows(u, s):
            return u[:, s, CONV_K - 1 + SEQ:UW].rearrange("p (b f) -> p b f", f=CONV_K)

        u_rows = u6[:, :, CONV_K - 1 + SEQ:UW].rearrange("p s (b f) -> p s b f", f=CONV_K)
        xbc_s = xbc[:, :, SEQ:CVW].rearrange("p s (b f) -> p s b f", f=CONV_K)[:, :, :, CONV_K - 1]
        seg_v = seg_b[:, :].rearrange("p (h i) -> p h i", h=4)
        dec_f = dec.rearrange("p u h i -> p u (h i)")
        diag_f = diag.rearrange("p h i -> p (h i)")
        bc_f = bc.rearrange("p i b n -> p i (b n)")

        def ln_column(n, bias, m):
            at = C_LN + 2 * KT * n + KT * bias + m
            return par[:, at:at + 1]

        def window_sums(e, i, a, b, signal, count):
            src, width = poolu[:, 4 * i:4 * i + 4, 0:16 + SEQ], 1
            while width < WINDOWS[i]:
                dst, lo = (b if src is a else a), 2 * width - 1
                e.tensor_tensor(dst[:, :, lo:16 + SEQ], src[:, :, lo:16 + SEQ],
                                src[:, :, lo - width:16 + SEQ - width], ALU.add).then_inc(signal, 1)
                e.wait_ge(signal, count())
                src, width = dst, 2 * width
            return src

        block = ctx.enter_context(nc.Block())

        @block.sync
        def _(sp):
            def load(src, q, off, tiles=HT):
                wait(sp, lo_ready, 4 * q + off - RING + 1)
                sp.dma_start(raw[:, off % RING, 0:tiles * P], src).then_inc(raw_landed[off % RING], 16)

            def slab(src, q, off):
                load(src[:, 0:HT * P], q, off)
                load(src[:, HT * P:2 * HT * P], q, off + 1)

            def iteration(g, lag):
                q = q_of(g, lag)
                for kind, i, off in slots(lag):
                    if kind == "w":
                        if lag:
                            slab(A["w_branch"][g - 1, i], q, off)
                    elif lag or (kind, i) != ("s", 0):
                        slab(A["w_in"][g, {"s": 0, "z": CT, "p": CT + GT}[kind] + i], q, off)

            def load_x(c):
                sp.dma_start(ya[:, 4 * c:4 * c + 4, :], A["x"][:, 4 * c:4 * c + 4, :]).then_inc(x_in[c], 16)

            half_slab = [slice(h * HT * P, (h + 1) * HT * P) for h in range(2)]
            load(A["w_dt"][:, half_slab[0]], 0, 0)
            load_x(0)
            load_x(1)
            load(A["w_dt"][:, half_slab[1]], 0, 1)
            load_x(2)
            load_x(3)
            sp.dma_start(par, A["params"]).then_inc(par_in, 16)
            for h in range(2):
                load(A["w_in"][0, 0, :, half_slab[h]], 0, FIRST_HALF + h)
            sp.dma_start(con, A["constants"]).then_inc(con_in, 16)
            sp.dma_start(scb, A["conv_rows"]).then_inc(scb_in, 16)
            iteration(0, False)
            with sp.Fori(1, G) as g:
                iteration(g, True)
            for j in range(4):
                slab(A["w_gate"][j], Q_EARLY, 2 + 2 * j)
            for i in range(GT):
                slab(A["w_branch"][G - 1, i], Q_TAIL, 2 + 2 * i)
            for i in range(4):
                slab(A["w_pool"][i], Q_POOL, 2 + 2 * i)
            with sp.Fori(1, KT // 2) as i:
                for j in range(4):
                    slab(A["w_gate"][4 * i + j], Q_GATE + 2 * i, 2 + 2 * j)
            with sp.Fori(0, KT // 4) as i:
                for j in range(4):
                    slab(A["w_out"][4 * i + j], Q_OUT + 2 * i, 2 + 2 * j)
            with sp.Fori(0, JF) as j:
                for w in range(2):
                    slab(A["w_up"][j, w], Q_UP + j, 2 + 2 * w)
            with sp.Fori(0, KT // 4) as i:
                for j in range(4):
                    at = 0
                    for n, tiles in enumerate(DOWN_TILES):
                        load(A["w_down"][4 * i + j, :, at * P:(at + tiles) * P], Q_DOWN + 6 * i, 2 + 6 * j + n, tiles)
                        at += tiles
            for c in range(4):
                part = slice(4 * c, 4 * c + 4)
                sp.wait_ge(y_even, 2 * c + 2)
                sp.wait_ge(y_odd, KT // 2 + 2 * c + 2)
                sp.dma_start(O["y"][:, part], res[:, part]).then_inc(y_stored, 16)

        @block.gpsimd
        def _(pool):
            def load_state(g, i):
                slot, turn = i % 2, 2 * g + i // 2
                wait(pool, st_out[slot], 16 * turn)
                wait(pool, ty_ready, 4 * g + i - 1)
                pool.dma_start(st[:, slot].rearrange("p b t n -> p (b t n)"),
                               A["state"][g, i]).then_inc(st_in[slot], 16)

            pool.wait_ge(xlo_ready, 4)
            pool.memset(ya, 0.0).then_inc(ya_zeroed, 1)

            def iteration(g, lag):
                wait(pool, conv_done, 24 * g)
                wait(pool, ust_done, g)
                pool.wait_ge(scb_in, 16)
                pool.tensor_copy(u_rows[:, :, :, 0:3], scb[:, g]).then_inc(ubuf_ready, 1)
                load_state(g, 0)
                load_state(g, 1)
                if not lag:
                    pool.wait_ge(con_in, 16)
                    pool.wait_ge(dt_dve, DT_TOK)
                for u in range(4):
                    wait(pool, bc_mm, 4 * g)
                    wait(pool, seg_mm, 4 * g + u)
                    pool.tensor_tensor(diag, tri.unsqueeze(1).to_broadcast([P, 4, P]),
                                       tok[:, 2 + u // 2, bass.ds(HG * g + 4 * (u % 2), 4)].unsqueeze(2)
                                       .to_broadcast([P, 4, P]), ALU.mult).then_inc(t_ready, 1)
                pool.wait_ge(acc_act, 12 * g + CT)
                pool.wait_ge(ubuf_ready, g + 1)
                pool.tensor_copy(cpo[:, g], u6[:, :, SEQ:SEQ + 3])
                pool.tensor_copy(scb[:, g], u_rows[:, :, :, 1:4]).then_inc(ust_done, 1)
                pool.wait_ge(xbc_ready, 2 * g + 1)
                for i in range(4):
                    wait(pool, seg_mm, 4 * g + 4)
                    wait(pool, bc_mm, 4 * g + i)
                    pool.tensor_tensor(diag, ident.unsqueeze(1).to_broadcast([P, 4, P]),
                                       xbc_s[:, i // 2, 4 * (i % 2):4 * (i % 2) + 4].unsqueeze(2)
                                       .to_broadcast([P, 4, P]), ALU.mult).then_inc(dg_ready, 1)
                pool.wait_ge(xbc_ready, 2 * g + 2)
                pool.wait_ge(exps_ready, 2 * g + 2)
                steps = 9 * g
                pool.tensor_tensor(dx, xbc_s[:, 2:CT].rearrange("p t b -> p b t"),
                                   exps[:, :, 0:NS].rearrange("p t b -> p b t"), ALU.mult).then_inc(pool_step, 1)
                pool.wait_ge(bc_ready, 4 * g + 4)
                pool.wait_ge(pool_step, steps + 1)
                for i in range(4):
                    slot = i % 2
                    pool.wait_ge(st_in[slot], 32 * g + 16 * (i // 2) + 16)
                    sv = st[:, slot]
                    da = exps[:, :, NS + 2 * i:NS + 2 * i + 2].rearrange("p t b -> p b t")
                    pool.tensor_tensor(sv, sv, da.unsqueeze(3).to_broadcast([P, 2, GT, P]),
                                       ALU.mult).then_inc(pool_step, 1)
                    rows_b = bc[:, i // 2, 2 * (i % 2):2 * (i % 2) + 2].unsqueeze(2).to_broadcast([P, 2, GT, P])
                    rows_c = bc[:, 2 + i // 2, 2 * (i % 2):2 * (i % 2) + 2].unsqueeze(2).to_broadcast([P, 2, GT, P])
                    wait(pool, snew, 4 * g + i)
                    pool.tensor_tensor(tm, rows_b, dx[:, 2 * i:2 * i + 2].unsqueeze(3).to_broadcast([P, 2, GT, P]),
                                       ALU.mult).then_inc(pool_step, 1)
                    if 1 <= i < 3:
                        load_state(g, i + 1)
                    pool.wait_ge(pool_step, steps + 1 + 2 * (i + 1))
                    pool.tensor_tensor(sv, sv, tm, ALU.add).then_inc(snew, 1)
                    wait(pool, red_done, 4 * g + i)
                    pool.wait_ge(snew, 4 * g + i + 1)
                    pool.tensor_tensor(ty, sv, rows_c, ALU.mult).then_inc(ty_ready, 1)
                    pool.dma_start(O["ssm_s"][g, i], sv.rearrange("p b t n -> p (b t n)")).then_inc(st_out[slot], 16)
                pool.wait_ge(st1_ready, g + 1)
                pool.dma_start(O["ssm_p"][g], s1).then_inc(s1_out, 16)

            iteration(0, False)
            with pool.Fori(1, G) as g:
                iteration(g, True)

            pool.wait_ge(s1_out, 16 * G)
            for slot in range(2):
                pool.wait_ge(st_out[slot], 32 * G)
            pool.wait_ge(red_done, 4 * G)
            pool.dma_start(spb, A["pool_rows"]).then_inc(spb_in, 16)
            pool.wait_ge(ust_done, G)
            pool.dma_start(O["conv_s"], scb).then_inc(conv_out, 16)
            pool.dma_start(O["conv_p"], cpo).then_inc(conv_out, 16)
            pool.memset(rsum, 0.0).then_inc(rsum_done, 1)
            pool.wait_ge(y3_ready, 4 * G)
            added = iter(range(1, 5))
            assert window_sums(pool, 3, qa, qb, widest_sum, lambda: next(added)) is qb
            pool.wait_ge(pool_rows, 2)
            pool.dma_start(O["pool_s"], spb).then_inc(pool_out, 16)
            pool.dma_start(O["pool_p"], ppo).then_inc(pool_out, 16)

            def sum_rows(base):
                with pool.Fori(0, KT) as m:
                    pool.wait_ge(res_ready, base + m + 1)
                    pool.wait_ge(rsum_done, base + base // KT + m + 1)
                    pool.tensor_tensor(rsum, rsum, res[:, m], ALU.add).then_inc(rsum_done, 1)

            sum_rows(0)
            pool.wait_ge(conv_out, 32)
            pool.wait_ge(pool_out, 32)
            pool.wait_ge(mean_mm, 1)
            pool.memset(rsum, 0.0).then_inc(rsum_done, 1)
            pool.memset(fpo, 0.0).then_inc(fst_done, 1)
            pool.dma_start(sfb, A["ffn_rows"]).then_inc(sfb_in, 16)

            def low_of_odd(m):
                pool.wait_ge(x1hi_ready, m + 1)
                pool.tensor_tensor(x1lo[:, m], res[:, m], x1hi[:, m].bitcast(F32), ALU.subtract).then_inc(x1lo_odd, 1)

            def odd_tiles(n):
                pool.wait_ge(lnr_ready, n + 1)
                for m in range(1, KT, 2):
                    pool.tensor_tensor(res[:, m], res[:, m], lnr[:, 3], ALU.mult).then_inc(odd_normed, 1)
                    if n == 0 and m >= 5:
                        low_of_odd(m - 4)
                if n == 0:
                    for m in (KT - 3, KT - 1):
                        low_of_odd(m)

            odd_tiles(0)
            pool.wait_ge(sfb_in, 16)
            uf_rows = uf[:, :, FFN_K - 1 + SEQ:FW].rearrange("p w (b f) -> p w b f", f=FFN_K)
            with pool.Fori(0, JF) as j:
                pool.wait_ge(fconv, 6 * j + 1)
                pool.wait_ge(fst_done, j + 1)
                pool.wait_ge(sfb_in, 16)
                pool.tensor_copy(uf_rows[:, :, :, 0:2], sfb[:, j]).then_inc(fbuf_ready, 1)
                pool.wait_ge(acc_act, ACT_UP + 2 * j + 2)
                pool.wait_ge(fbuf_ready, j + 1)
                pool.tensor_copy(fpo[:, j], uf[:, :, SEQ:SEQ + 2])
                pool.tensor_copy(sfb[:, j], uf_rows[:, :, :, 1:3]).then_inc(fst_done, 1)
            pool.wait_ge(fst_done, JF + 1)
            pool.dma_start(O["ffn_s"], sfb).then_inc(stored, 16)
            pool.dma_start(O["ffn_p"], fpo).then_inc(stored, 16)
            sum_rows(KT)
            odd_tiles(1)
            pool.wait_ge(stored, 2 * 16)
            pool.wait_ge(y_stored, 4 * 16)

        @block.tensor
        def _(pe):
            def half(q, off, tiles, hi, lo, bank_wait=None, tile_wait=None):
                slot = off % RING
                pe.wait_ge(lo_ready, 4 * q + off + 1)
                for n, (bank, k, first, last) in enumerate(tiles):
                    if first and bank_wait is not None:
                        bank_wait(n)
                    if tile_wait is not None:
                        tile_wait(k)
                    out = acc[bank][:, 0:T]
                    w_hi, w_lo = (w[:, slot, n * P:(n + 1) * P] for w in (whi, wlo))
                    pe.matmul(out, w_hi, hi[:, k], start=first, stop=False)
                    pe.matmul(out, w_hi, lo[:, k], start=False, stop=False)
                    ins = pe.matmul(out, w_lo, hi[:, k], start=False, stop=last)
                ins.then_inc(half_used, 1)

            def slab(q, off, bank, hi, lo, bank_wait, tile_wait=None):
                half(q, off, [(bank, k, k == 0, False) for k in range(HT)], hi, lo, bank_wait, tile_wait)
                half(q, off + 1, [(bank, HT + k, False, k == HT - 1) for k in range(HT)], hi, lo, None, tile_wait)

            def slab_of_4(q, off, banks, hi, lo, bank_wait):
                for h in range(2):
                    half(q, off + h, [(banks[2 * h + n // 4], n % 4, n % 4 == 0, n % 4 == 3) for n in range(HT)],
                         hi, lo, lambda n, h=h: bank_wait(2 * h + n // 4))

            def branch(q, off, i, before, first_wait):
                def bank_wait(r):
                    if i == 0:
                        first_wait(r)
                    else:
                        pe.wait_ge(acc_dve, before + 4 * (i - 1) + r + 1)
                return bank_wait

            for c in range(4):
                pe.wait_ge(xlo_ready, c + 1)
                if c % 2 == 0:
                    pe.wait_ge(lo_ready, c // 2 + 1)
                for k in range(4 * c, 4 * c + 4):
                    w_hi, w_lo = (w[:, k // HT, (k % HT) * P:(k % HT + 1) * P] for w in (whi, wlo))
                    pe.matmul(misc[:, 0:T], w_hi, xhi[:, k], start=k == 0, stop=False)
                    pe.matmul(misc[:, 0:T], w_hi, xlo[:, k], start=False, stop=False)
                    ins = pe.matmul(misc[:, 0:T], w_lo, xhi[:, k], start=False, stop=k == KT - 1)
                if c % 2 == 1:
                    ins.then_inc(half_used, 1)

            def dt_turned():
                pe.wait_ge(con_in, 16)
                pe.wait_ge(dt_dve, DT_DONE)
                for n, row in enumerate((0, 0, 1, 1)):
                    ins = pe.transpose(seg_b[:, 64 * n:64 * n + 64], dts[0:64, row, P * (n % 2):P * (n % 2 + 1)],
                                       ident[0:64, 0:64])
                ins.then_inc(dt_mm, 1)

            def dt_sums():
                pe.wait_ge(dt_dve, DT_TOK)
                da = tok[:, 2:4, :].rearrange("p c h -> p (c h)")
                pe.matmul(tp_b[:, 0:P], tri, da, start=True, stop=True)
                pe.matmul(tp_b[:, P:2 * P], ones, da, start=True, stop=True)
                pe.matmul(yd_b[0:64, 0:P], tok[:, 3, :], tri, start=True, stop=True).then_inc(dt_mm, 1)

            def per_channel(g):
                pe.wait_ge(exr_ready, g + 1)
                wait(pe, yo_read, g)
                wait(pe, ms_ready, g)
                for t in range(GT):
                    bank = (tp_b, misc)[t // 2]
                    ins = pe.matmul(bank[:, EW * (t % 2):EW * (t % 2 + 1)], con[:, K_E + P * t:K_E + P * (t + 1)],
                                    exg, start=True, stop=True)
                ins.then_inc(exp_mm, 1)

            def square_sum(turn):
                pe.wait_ge(vsq_ready, turn)
                pe.wait_ge(st1_ready, turn)
                pe.matmul(misc[:, 0:T], ones, rs[:, 1], start=True, stop=True).then_inc(ssq_mm, 1)

            def decay(g, u):
                pe.wait_ge(t_ready, 4 * g + u + 1)
                wait(pe, dec_ready, 4 * g + u)
                if u == 0:
                    wait(pe, yd_read, 8 * g)
                pe.matmul(seg_b[:, :], low, diag_f, start=True, stop=True).then_inc(seg_mm, 1)

            def rows(g, i):
                pe.wait_ge(dg_ready, 4 * g + i + 1)
                wait(pe, bc_ready, 4 * g + i)
                if i == 0:
                    wait(pe, yd_read, 8 * g)
                pe.matmul(yd_b[:, :], ones, diag_f, start=True, stop=True).then_inc(bc_mm, 1)

            def cb(g):
                pe.wait_ge(xbc_ready, 2 * g + 1)
                pe.wait_ge(exps_ready, 2 * g + 2)
                wait(pe, ms_ready, g)
                for c in range(2):
                    part = slice(c * P, (c + 1) * P)
                    pe.matmul(misc[:, part], xbc[:, 0, part], xbc[:, 1, part], start=True, stop=True)
                for c in range(2):
                    ins = pe.transpose(misc[:, (2 + c) * P:(3 + c) * P], xbc[:, 0, c * P:(c + 1) * P], ident)
                ins.then_inc(cb_mm, 1)

            def x_turned(g, c):
                pe.wait_ge(xbc_ready, 2 * g + 2)
                pe.wait_ge(exps_ready, 2 * g + 2)
                if c:
                    pe.wait_ge(xdt_ready, 4 * g + 2)
                for t in range(GT):
                    ins = pe.transpose(tp_b[:, t * P:(t + 1) * P], xbc[:, 2 + t, c * P:(c + 1) * P], ident)
                ins.then_inc(xt_mm, 1)

            def state(g, c):
                pe.wait_ge(xdt_ready, 4 * g + 2 * c + 2)
                pe.wait_ge(btok_ready, g + 1)
                pe.wait_ge(cbm_ready, g + 1)
                if c:
                    pe.wait_ge(s0_ready, g + 1)
                pe.matmul(misc[:, :], btok[:, c], xde[:, c], start=True, stop=True).then_inc(st_mm, 1)

            def y_heads(g, c):
                pe.wait_ge(m_ready, 4 * g + 2 * c + 2)
                pe.wait_ge(xdt_ready, 4 * g + 2 * c + 2)
                pe.wait_ge(bc_ready, 4 * g + 4)
                if c:
                    pe.wait_ge(yd_read, 8 * g + 4)
                for t in range(GT):
                    bank = (yd_b, seg_b)[t // 2]
                    ins = pe.matmul(bank[:, 256 * (t % 2):256 * (t % 2 + 1)], xdt[:, c, t * P:(t + 1) * P],
                                    dec[:, 2 * c + t // 2, 2 * (t % 2):2 * (t % 2) + 2].rearrange("p h i -> p (h i)"),
                                    start=True, stop=True)
                ins.then_inc(yd_mm, 1)

            def y_state(g):
                pe.wait_ge(s0_ready, g + 1)
                pe.wait_ge(xdt_ready, 4 * g + 4)
                for t in range(GT):
                    ins = pe.matmul(tp_b[:, t * P:(t + 1) * P], s0[:, t * P:(t + 1) * P], xbc[:, 1, P:2 * P],
                                    start=True, stop=True)
                ins.then_inc(yo_mm, 1)

            def iteration(g, lag):
                q = q_of(g, lag)
                seen = 0
                for kind, i, off in slots(lag):
                    if kind == "w":
                        if lag:
                            if i == 0:
                                pe.wait_ge(ylo_ready, g)
                            slab_of_4(q, off, [(2 + r) % 4 for r in range(4)], yhi, ylo,
                                      branch(q, off, i, GT * GT * (g - 1),
                                             lambda r: pe.wait_ge(acc_act, 12 * g + 3 + r)))
                    else:
                        if kind == "z" and lag:
                            free = (acc_dve, GT * GT * (g - 1) + 13 + i)
                        else:
                            free = (acc_act, 12 * g - 3 + seen)
                        slab(q, off, seen % 4, xhi, xlo, lambda n: wait(pe, *free))
                        seen += 1
                    if kind == "s":
                        if not lag and i == 1:
                            dt_turned()
                        elif not lag and i == 2:
                            dt_sums()
                        elif i == 2:
                            square_sum(g)
                        elif i == 4:
                            per_channel(g)
                        if i >= 2:
                            decay(g, i - 2)
                    elif kind == "w":
                        rows(g, i)
                        if i == 1:
                            cb(g)
                        elif i >= 2:
                            x_turned(g, i - 2)
                    elif kind == "z":
                        if i == 0:
                            state(g, 0)
                        elif i == 1:
                            y_heads(g, 0)
                        elif i == 2:
                            state(g, 1)
                            y_heads(g, 1)
                        else:
                            y_state(g)

            iteration(0, False)
            with pe.Fori(1, G) as g:
                iteration(g, True)

            for j in range(4):
                slab(Q_EARLY, 2 + 2 * j, j, xhi, xlo, lambda n, j=j: pe.wait_ge(acc_act, 12 * G + j - 3))
                if j == 1:
                    square_sum(G)
            pe.wait_ge(ylo_ready, G)
            for i in range(GT):
                slab_of_4(Q_TAIL, 2 + 2 * i, range(4), yhi, ylo,
                          branch(None, None, i, GT * GT * (G - 1), lambda r: pe.wait_ge(acc_act, 12 * G + 1 + r)))
            for i in range(4):
                pe.wait_ge(plo_ready, i + 1)
                slab_of_4(Q_POOL, 2 + 2 * i, range(4), phi[:, i % 2], plo[i % 2],
                          (lambda r: pe.wait_ge(acc_dve, DVE_OUT - 3 + r)) if i == 0 else
                          (lambda r, i=i: pe.wait_ge(acc_act, ACT_POOL + 4 * i - 3 + r)))
            with pe.Fori(1, KT // 2) as i:
                for j in range(4):
                    slab(Q_GATE + 2 * i, 2 + 2 * j, j, xhi, xlo,
                         lambda n, j=j: pe.wait_ge(acc_act, ACT_GATE + 4 * i + j - 3))

            def out_bank(i, j):
                pe.wait_ge(acc_act, ACT_UP + j - 3)
                pe.wait_ge(acc_dve, DVE_OUT + 4 * i + j - 3)

            with pe.Fori(0, KT // 4) as i:
                for j in range(4):
                    slab(Q_OUT + 2 * i, 2 + 2 * j, j, mhi, mlo, lambda n, j=j: out_bank(i, j),
                         (lambda k: pe.wait_ge(mlo_ready, {KT - 2: KT - 1, KT - 1: KT}.get(k, KT - 2))
                          if k in (0, KT - 2, KT - 1) else None) if j == 0 else None)

            def layer_norm(n):
                pe.wait_ge(rsum_done, (n + 1) * (KT + 1))
                pe.matmul(seg_b[:, 0:T], ones, rsum, start=True, stop=True).then_inc(mean_mm, 1)
                for c in range(4):
                    pe.wait_ge(sq_ready, 4 * n + c + 1)
                    for t in range(4):
                        ins = pe.matmul(tp_b[:, 0:T], ones, lsq[:, c % 2, t], start=c + t == 0, stop=c + t == 6)
                    ins.then_inc(sq_mm, 1)

            layer_norm(0)

            def up(j, tile_wait=None):
                for w in range(2):
                    slab(Q_UP + j, 2 + 2 * w, w, x1hi, x1lo, lambda n: pe.wait_ge(acc_act, ACT_UP + 2 * j + w - 1),
                         None if w else tile_wait)

            up(0, lambda k: pe.wait_ge((x1lo_even, x1lo_odd)[k % 2], k // 2 + 1))
            with pe.Fori(1, JF) as j:
                up(j)
            pe.wait_ge(acc_act, ACT_UP + 2 * JF)
            with pe.Fori(0, KT // 4) as i:
                for j in range(4):
                    k = 0
                    for n, tiles in enumerate(DOWN_TILES):
                        if j == 0 and n in (0, 5):
                            pe.wait_ge(flo_ready, JF if n else JF - 1)
                        half(Q_DOWN + 6 * i, 2 + 6 * j + n,
                             [(j, k + r, k + r == 0, k + r == JF - 1) for r in range(tiles)], hhi, hlo,
                             lambda n, j=j: pe.wait_ge(acc_dve, DVE_DOWN + 4 * i + j - 3))
                        k += tiles
            layer_norm(1)

        @block.scalar
        def _(act):
            def split(q, off, tiles=HT):
                slot = off % RING
                act.wait_ge(raw_landed[slot], 16 * (q + off // RING + 1))
                wait(act, half_used, 4 * q + off - RING + 1)
                part = slice(0, tiles * P)
                act.activation(whi[:, slot, part], raw[:, slot, part], ACT.Copy).then_inc(hi_ready, 1)

            def slab_done(q, off):
                split(q, off + RING)
                act.wait_ge(half_used, 4 * q + off + 2)

            for c in range(4):
                if c % 2 == 0:
                    split(0, c // 2)
                part = slice(4 * c, 4 * c + 4)
                act.wait_ge(x_in[c], 16)
                act.activation(xhi[:, part], ya[:, part], ACT.Copy).then_inc(xhi_ready, 1)
            split(0, 2)
            split(0, 3)

            act.wait_ge(par_in, 16)
            act.wait_ge(dt_dve, 4)
            act.activation(dts[0:64, 4], dts[0:64, 3], ACT.Exp, scale=-1.0).then_inc(dt_act, 1)
            act.activation(hcol[0:64, 0:1], par[0:64, C_HEAD + 1:C_HEAD + 2], ACT.Exp).then_inc(dt_act, 1)
            split(0, 4)
            split(0, 5)

            def dt_at_samples():
                act.wait_ge(dt_dve, DT_DONE)
                act.activation(exr[0:64, NS:2 * NS], dts[0:64, 1, SEQ:T], ACT.Exp).then_inc(dt_act, 1)

            def dt_exponentials():
                act.wait_ge(dt_mm, 2)
                act.activation(exr[0:64, 2 * NS + 2:EW], yd_b[0:64, 0:P], ACT.Exp).then_inc(dt_act, 1)
                act.wait_ge(dt_dve, DT_TOK + 2)
                act.activation(ctot.rearrange("p c h -> p (c h)"), tp_b[:, P:2 * P], ACT.Exp).then_inc(dt_act, 1)
                act.activation(fe.rearrange("p c h -> p (c h)"), fe.rearrange("p c h -> p (c h)"),
                               ACT.Exp).then_inc(dt_act, 1)

            def silu_of_convolved(g, part, steps):
                act.wait_ge(conv_done, 24 * g + steps)
                act.activation(xbc[:, part], xbc[:, part], ACT.Silu).then_inc(xbc_ready, 1)

            def iteration(g, lag):
                q = q_of(g, lag)
                seen = 0
                for kind, i, off in slots(lag):
                    if not lag and (kind, i) == ("s", 2):
                        dt_at_samples()
                    if not lag and (kind, i) == ("s", 4):
                        dt_exponentials()
                    if off is not None:
                        split(q, off + RING)
                        if lag and (kind, i) == ("s", 3):
                            act.wait_ge(ms_ready, g)
                            act.activation(rs[:, 1], rs[:, 0], ACT.Sqrt).then_inc(std_ready, 1)
                        elif lag and (kind, i) == ("s", 4):
                            act.wait_ge(y3_ready, 4 * g)
                            act.activation(yhi, y3, ACT.Copy).then_inc(yhi_ready, 1)
                        act.wait_ge(half_used, 4 * q + off + 2)
                    if kind == "s":
                        bank = acc[seen % 4]
                        if i == 0:
                            wait(act, conv_done, 24 * g)
                            wait(act, ust_done, g)
                        act.activation(u6[:, i, CONV_K - 1:CONV_K - 1 + SEQ], bank[:, 0:SEQ], ACT.Copy)
                        act.activation(u_rows[:, i, :, CONV_K - 1], bank[:, SEQ:T], ACT.Copy).then_inc(acc_act, 1)
                        seen += 1
                        split(q, off + RING + 1)
                        if i == 4:
                            act.wait_ge(exp_mm, g + 1)
                            wait(act, ty_ready, 4 * g)
                            wait(act, vsq_ready, g)
                            for h, part in enumerate((tp_b, misc)):
                                act.activation(exps[:, 2 * h:2 * h + 2], part[:, 0:2 * EW].rearrange(
                                    "p (t e) -> p t e", t=2), ACT.Copy).then_inc(exps_ready, 1)
                        if i >= 2:
                            u = i - 2
                            act.wait_ge(seg_mm, 4 * g + u + 1)
                            act.activation(dec[:, u].rearrange("p h i -> p (h i)"), seg_b[:, :],
                                           ACT.Exp).then_inc(dec_ready, 1)
                        if i == 5:
                            silu_of_convolved(g, slice(0, 2), 8)
                    elif kind == "w":
                        if lag:
                            split(q, off + RING + 1)
                        if i == 0:
                            silu_of_convolved(g, slice(2, CT), 24)
                        act.wait_ge(bc_mm, 4 * g + i + 1)
                        wait(act, ty_ready, 4 * g)
                        act.activation(bc_f[:, i], yd_b[:, :], ACT.Copy).then_inc(bc_ready, 1)
                        if i == 1:
                            act.wait_ge(cb_mm, g + 1)
                            act.wait_ge(cbm_ready, g + 1)
                            act.activation(btok.rearrange("p c n -> p (c n)"), misc[:, 2 * P:4 * P],
                                           ACT.Copy).then_inc(btok_ready, 1)
                    elif kind == "z":
                        wait(act, vsq_ready, g)
                        act.activation(zs[:, i], acc[seen % 4][:, 0:T], ACT.Silu).then_inc(acc_act, 1)
                        seen += 1
                        split(q, off + RING + 1)
                        if i == 0:
                            act.wait_ge(st_mm, 2 * g + 1)
                            wait(act, st1_ready, g)
                            act.activation(s0, misc[:, :], ACT.Copy).then_inc(s0_ready, 1)
                        elif i < 3:
                            c = i - 1
                            act.wait_ge(yd_mm, 2 * g + i)
                            wait(act, y3_ready, 4 * g)
                            for b, bank in enumerate((yd_b, seg_b)):
                                for h in range(2):
                                    rows = slice(64 * h, 64 * h + 64)
                                    act.activation(yt[rows, 2 * b:2 * b + 2, c * P:(c + 1) * P],
                                                   bank[rows, :].rearrange("p (t h i) -> p t h i", t=2, h=2)[:, :, h],
                                                   ACT.Copy).then_inc(yd_read, 1)
                    else:
                        act.activation(poolu[:, 2 * g + i, 16:PW], acc[seen % 4][:, 0:T], ACT.Copy).then_inc(acc_act, 1)
                        seen += 1
                        split(q, off + RING + 1)

            iteration(0, False)
            with act.Fori(1, G) as g:
                iteration(g, True)

            def gate(q, i, j):
                slab_done(q, 2 + 2 * j)
                if i is not None:
                    act.wait_ge(mx_step, 4 * i + 2 * (j // 2) + 1)
                act.activation(sg[:, j], acc[j][:, 0:T], ACT.Sigmoid,
                               bias=par[:, bass.ds(C_GATE + (0 if i is None else 4 * i) + j, 1)]).then_inc(acc_act, 1)
                split(q, 2 + 2 * j + RING + 1)

            def high_of_mix(m, a):
                act.wait_ge(mx_ready, m + 1)
                act.activation(mhi[:, m], mx[:, a, 0], ACT.Copy).then_inc(mhi_ready, 1)

            for j in range(4):
                if j == 2:
                    act.wait_ge(ms_ready, G)
                    act.activation(rs[:, 1], rs[:, 0], ACT.Sqrt).then_inc(std_ready, 1)
                elif j == 3:
                    act.wait_ge(y3_ready, 4 * G)
                    act.activation(yhi, y3, ACT.Copy).then_inc(yhi_ready, 1)
                gate(Q_EARLY, None, j)

            def round_pooled(i):
                act.wait_ge(pooled, i + 1)
                if i >= 2:
                    act.wait_ge(half_used, 4 * Q_POOL + 2 + 2 * (i - 1))
                act.activation(phi[:, i % 2], pp, ACT.Copy).then_inc(phi_ready, 1)

            for i in range(GT):
                if i == 1:
                    round_pooled(0)
                split(Q_TAIL, 2 + 2 * i + RING)
                if i == 2:
                    round_pooled(1)
                split(Q_TAIL, 2 + 2 * i + RING + 1)
            for i in range(4):
                for h in range(2):
                    split(Q_POOL, 2 + 2 * i + h + RING)
                    act.wait_ge(half_used, 4 * Q_POOL + 3 + 2 * i + h)
                    for r in range(2 * h, 2 * h + 2):
                        m = 4 * i + r
                        act.activation(yb[:, m], acc[r][:, 0:T], ACT.Copy,
                                       scale=par[:, C_PSC + m:C_PSC + m + 1]).then_inc(acc_act, 1)
                if i < 2:
                    round_pooled(i + 2)
            act.wait_ge(conv_out, 32)
            for m in range(2):
                high_of_mix(m, m)
            with act.Fori(1, KT // 2) as i:
                for j in range(4):
                    gate(Q_GATE + 2 * i, i, j)
                    if j % 2:
                        high_of_mix(2 * i + j // 2, j // 2)
            with act.Fori(0, KT // 4) as i:
                for n in range(8):
                    split(Q_OUT + 2 * i, 2 + n + RING)

            def layer_norm(n):
                for c in range(4):
                    act.wait_ge(rc_ready, 4 * n + c + 1)
                    wait(act, sq_mm, 4 * n + c - 1)
                    act.activation(lsq[:, c % 2], res[:, 4 * c:4 * c + 4], ACT.Square).then_inc(sq_ready, 1)
                act.wait_ge(var_ready, n + 1)
                act.activation(lnr[:, 2], lnr[:, 1], ACT.Sqrt).then_inc(lnstd, 1)

            def weigh_odd(n, m):
                act.wait_ge(odd_normed, (KT * n + m + 1) // 2)
                act.activation(res[:, m], res[:, m], ACT.Identity, bias=ln_column(n, 1, m),
                               scale=ln_column(n, 0, m)).then_inc(y_odd, 1)

            layer_norm(0)
            act.wait_ge(pool_out, 32)
            for m in range(KT):
                if m % 2:
                    weigh_odd(0, m)
                    act.wait_ge(y_odd, m // 2 + 1)
                    act.activation(x1hi[:, m], res[:, m], ACT.Copy).then_inc(x1hi_ready, 1)
                else:
                    act.wait_ge(even_normed, m // 2 + 1)
                    act.activation(x1hi[:, m], res[:, m], ACT.Identity, bias=ln_column(0, 1, m)).then_inc(x1hi_ready, 1)

            def gated_high(j):
                act.wait_ge(fh_ready, 2 * j + 2)
                act.activation(hhi[:, j], hh, ACT.Copy).then_inc(fhi_ready, 1)

            def up(j, first):
                for w in range(2):
                    q, off = Q_UP + j, 2 + 2 * w
                    split(q, off + RING)
                    if w:
                        act.wait_ge(fconv, 6 * j + 4)
                        act.activation(fc[:, 0], fc[:, 0], ACT.Silu).then_inc(fsilu, 1)
                    act.wait_ge(half_used, 4 * q + off + 2)
                    wait(act, fconv, 6 * j - 2 + 3 * w)
                    act.wait_ge(fst_done, j + 1)
                    act.activation(uf[:, w, FFN_K - 1:FFN_K - 1 + SEQ], acc[w][:, 0:SEQ], ACT.Copy)
                    act.activation(uf[:, w, FFN_K - 1 + SEQ:FW].rearrange("p (b f) -> p b f", f=FFN_K)[:, :, FFN_K - 1],
                                   acc[w][:, SEQ:T], ACT.Copy).then_inc(acc_act, 1)
                    split(q, off + RING + 1)
                    if not first and not w:
                        gated_high(j - 1)

            up(0, True)
            with act.Fori(1, JF) as j:
                up(j, False)
            gated_high(JF - 1)

            def down(i, last):
                for j in range(4):
                    for n in range(6):
                        if not (last and j == 3 and n >= 2):
                            split(Q_DOWN + 6 * i, 2 + 6 * j + n + RING, DOWN_TILES[(n + RING) % 6])

            with act.Fori(0, KT // 4 - 1) as i:
                down(i, False)
            down(KT // 4 - 1, True)
            layer_norm(1)
            for m in range(1, KT, 2):
                weigh_odd(1, m)

        @block.vector
        def _(dve):
            def split(q, off, tiles=HT):
                slot = off % RING
                dve.wait_ge(hi_ready, 4 * q + off + 1)
                part = slice(0, tiles * P)
                dve.tensor_tensor(wlo[:, slot, part], raw[:, slot, part], whi[:, slot, part].bitcast(F32),
                                  ALU.subtract).then_inc(lo_ready, 1)

            def head(row):
                return dts[0:64, row]

            chain = [0]

            def then(ins):
                ins.then_inc(dt_dve, 1)
                chain[0] += 1
                dve.wait_ge(dt_dve, chain[0])

            dve.memset(poolu[:, :, 0:16], 0.0)
            dve.memset(u6[:, :, 0:CONV_K - 1], 0.0).then_inc(zeroed, 1)
            for c in range(4):
                if c % 2 == 0:
                    split(0, c // 2)
                part = slice(4 * c, 4 * c + 4)
                dve.wait_ge(xhi_ready, c + 1)
                dve.tensor_tensor(xlo[:, part], ya[:, part], xhi[:, part].bitcast(F32),
                                  ALU.subtract).then_inc(xlo_ready, 1)

            def dt_argument():
                then(dve.memset(exr, 0.0))
                dve.wait_ge(half_used, 2)
                dve.wait_ge(par_in, 16)
                then(dve.tensor_scalar(head(2), misc[0:64, 0:T], par[0:64, C_HEAD:C_HEAD + 1], None, ALU.add))
                then(dve.tensor_scalar(head(1), head(2), 0.0, None, ALU.max))
                then(dve.scalar_tensor_tensor(out=head(3), in0=head(1), scalar=2.0, in1=head(2),
                                              op0=ALU.mult, op1=ALU.subtract))

            def dt_ratio():
                dve.wait_ge(dt_act, 1)
                then(dve.tensor_scalar(head(5), head(4), 2.0, None, ALU.add))
                then(dve.reciprocal(head(6), head(5)))
                then(dve.tensor_tensor(head(3), head(4), head(6), ALU.mult))
                then(dve.tensor_tensor(head(4), head(3), head(3), ALU.mult))

            def dt_series():
                then(dve.tensor_scalar(head(5), head(4), 1.0 / 17, None, ALU.mult))
                for k in range(7, 0, -1):
                    then(dve.scalar_tensor_tensor(out=head(5), in0=head(5), scalar=1.0 / (2 * k + 1), in1=head(4),
                                                  op0=ALU.add, op1=ALU.mult))

            def dt_and_da():
                then(dve.scalar_tensor_tensor(out=head(5), in0=head(5), scalar=1.0, in1=head(3),
                                              op0=ALU.add, op1=ALU.mult))
                then(dve.scalar_tensor_tensor(out=head(0), in0=head(5), scalar=2.0, in1=head(1),
                                              op0=ALU.mult, op1=ALU.add))
                dve.wait_ge(dt_act, 2)
                then(dve.tensor_scalar(hcol[0:64, 1:2], hcol[0:64, 0:1], -1.0, None, ALU.mult))
                then(dve.tensor_scalar(head(1), head(0), hcol[0:64, 1:2], None, ALU.mult))
                assert chain[0] == DT_DONE

            def dt_per_token():
                dve.wait_ge(dt_mm, 1)
                then(dve.tensor_copy(tok.rearrange("p r h -> p (r h)"), seg_b[:, 0:4 * N_HEADS]))
                assert chain[0] == DT_TOK

            acs_f, fe_f = (x.rearrange("p c h -> p (c h)") for x in (acs, fe))

            def dt_cumulative():
                dve.wait_ge(dt_mm, 2)
                then(dve.tensor_copy(acs_f, tp_b[:, 0:P]))
                then(dve.tensor_tensor(fe_f, tp_b[:, P:2 * P], acs_f, ALU.subtract))

            def dt_at_end():
                dve.wait_ge(dt_act, DT_ACT)
                then(dve.tensor_tensor(fe_f, fe_f, tok[:, 0:2].rearrange("p c h -> p (c h)"), ALU.mult))
                then(dve.tensor_copy(exr[0:64, 0:NS], dts[0:64, 0, SEQ:T]))
                then(dve.tensor_copy(exr[0:64, 2 * NS:2 * NS + 2],
                                     par[0:64, C_HEAD + 2:C_HEAD + 3].to_broadcast([64, 2])))

            split(0, 2)
            dt_argument()
            split(0, 3)
            dt_ratio()
            split(0, 4)
            split(0, 5)
            dt_series()
            DT_STEPS = {0: dt_and_da, 2: dt_per_token, 3: dt_cumulative, 4: dt_at_end}

            state = {"n": 0, "base": 0}

            def step():
                state["n"] += 1
                return state["base"] + state["n"]

            def convolve(g, tiles, done):
                for k in range(CONV_K):
                    for s in tiles:
                        u, x = u6[:, s, k:k + CVW], xbc[:, s]
                        tap = conv_w[:, g, s, k:k + 1]
                        if k == 0:
                            ins = dve.tensor_scalar(x, u, tap, conv_w[:, g, s, CONV_K:CONV_K + 1], ALU.mult, ALU.add)
                        else:
                            dve.wait_ge(conv_done, 24 * g + done - 1)
                            ins = dve.scalar_tensor_tensor(out=x, in0=u, scalar=tap, in1=x, op0=ALU.mult, op1=ALU.add)
                        ins.then_inc(conv_done, 1)
                        done += 1

            def normalise(g, turn):
                dve.wait_ge(ssq_mm, turn)
                dve.tensor_scalar(rs[:, 0], misc[:, 0:T], 1.0 / (GT * P), EPS, ALU.mult, ALU.add).then_inc(ms_ready, 1)
                dve.wait_ge(std_ready, turn)
                dve.reciprocal(rs[:, 0], rs[:, 1]).then_inc(rstd_ready, 1)
                dve.wait_ge(rstd_ready, turn)
                for t in range(GT):
                    dve.scalar_tensor_tensor(out=y3[:, t], in0=yt[:, t], scalar=norm_w[:, g, t:t + 1], in1=rs[:, 0],
                                             op0=ALU.mult, op1=ALU.mult).then_inc(y3_ready, 1)

            def low_of_y(turn):
                dve.wait_ge(yhi_ready, turn)
                dve.tensor_tensor(ylo, y3, yhi.bitcast(F32), ALU.subtract).then_inc(ylo_ready, 1)

            def branch(q, off, i, first_bank):
                for h in range(2):
                    split(q, off + h + RING)
                    dve.wait_ge(half_used, 4 * q + off + h + 1)
                    for r in range(2 * h, 2 * h + 2):
                        m = 4 * i + r
                        dve.tensor_tensor(ya[:, m], ya[:, m], acc[(first_bank + r) % 4][:, 0:T],
                                          ALU.add).then_inc(acc_dve, 1)

            def sample_sum(g, i):
                dve.wait_ge(ty_ready, 4 * g + i + 1)
                dve.tensor_reduce(yt[:, :, SEQ + 2 * i:SEQ + 2 * i + 2].rearrange("p t b -> p b t"), ty, AX_X,
                                  ALU.add).then_inc(red_done, 1)

            def gate_y(turn):
                sample_sum(turn - 1, 3)
                dve.wait_ge(red_done, 4 * turn)
                dve.tensor_tensor(yt[:, :, SEQ:T], yt[:, :, SEQ:T], sml[:, 0], ALU.add).then_inc(dve_step, 1)
                now = step()
                dve.wait_ge(acc_act, 12 * turn)
                dve.wait_ge(dve_step, now)
                dve.tensor_tensor(yt, yt, zs, ALU.mult).then_inc(dve_step, 1)
                now = step()
                dve.wait_ge(dve_step, now)
                dve.tensor_tensor(y3, yt, yt, ALU.mult).then_inc(dve_step, 1)
                now = step()
                dve.wait_ge(dve_step, now)
                dve.tensor_reduce(rs[:, 1], y3.rearrange("p t i -> p i t"), AX_X, ALU.add).then_inc(vsq_ready, 1)

            def mask_decays(g, c, half):
                u = 2 * c + half
                dve.wait_ge(cbm_ready, g + 1)
                dve.wait_ge(dec_ready, 4 * g + u + 1)
                dve.tensor_tensor(dec[:, u], dec[:, u], cbm[:, c].unsqueeze(1).to_broadcast([P, 4, P]),
                                  ALU.mult).then_inc(m_ready, 1)

            def heads(row, g):
                return row[:, bass.ds(HG * g, HG)].unsqueeze(2).to_broadcast([P, HG, HEAD_DIM])

            def by_head(x):
                return x.rearrange("p (h d) -> p h d", h=HG)

            def iteration(g, lag):
                q = q_of(g, lag)

                def heads_of_group():
                    wait(dve, exp_mm, g)
                    dve.tensor_scalar(exg, exr, con[:, bass.ds(K_MASK + g, 1)], None, ALU.mult).then_inc(exr_ready, 1)

                if lag:
                    heads_of_group()
                else:
                    dve.wait_ge(con_in, 16)
                    dve.wait_ge(zeroed, 1)
                for kind, i, off in slots(lag):
                    if kind == "w" and lag:
                        branch(q, off, i, 2)
                    elif off is not None:
                        dt_steps = DT_STEPS.get(i) if kind == "s" and not lag else None
                        split(q, off + RING)
                        if dt_steps:
                            dt_steps()
                            if i == 4:
                                dve.wait_ge(ya_zeroed, 1)
                                heads_of_group()
                        if (kind, i) == ("s", 3) and lag:
                            normalise(g - 1, g)
                        elif (kind, i) == ("s", 4) and lag:
                            low_of_y(g)
                        split(q, off + RING + 1)
                    if kind == "s":
                        if lag and i == 0:
                            gate_y(g)
                        if i % 2:
                            if i == 1:
                                dve.wait_ge(ubuf_ready, g + 1)
                                wait(dve, yo_mm, g)
                                wait(dve, pool_step, 9 * g)
                                wait(dve, ty_ready, 4 * g)
                            dve.wait_ge(acc_act, 12 * g + i + 1)
                            convolve(g, (i - 1, i), 4 * (i - 1))
                    elif kind == "w":
                        if i == 1:
                            dve.wait_ge(cb_mm, g + 1)
                            dve.tensor_tensor(cbm, misc[:, 0:2 * P].rearrange("p (c i) -> p c i", c=2),
                                              tri.unsqueeze(1).to_broadcast([P, 2, P]), ALU.mult).then_inc(cbm_ready, 1)
                            dve.wait_ge(cbm_ready, g + 1)
                        elif i >= 2:
                            c = i - 2
                            dve.wait_ge(xt_mm, 2 * g + c + 1)
                            dve.tensor_tensor(by_head(xdt[:, c]), by_head(tp_b[:, :]), heads(tok[:, c], g),
                                              ALU.mult).then_inc(xdt_ready, 1)
                            dve.tensor_tensor(by_head(xde[:, c]), by_head(tp_b[:, :]), heads(fe[:, c], g),
                                              ALU.mult).then_inc(xdt_ready, 1)
                            mask_decays(g, 0, c)
                    elif kind == "z":
                        if i < 2:
                            mask_decays(g, 1, i)
                            sample_sum(g, i)
                        if i == 2:
                            wait(dve, s1_out, 16 * g)
                            dve.wait_ge(s0_ready, g + 1)
                            dve.tensor_tensor(by_head(s1), by_head(s0), heads(ctot[:, 1], g),
                                              ALU.mult).then_inc(dve_step, 1)
                            now = step()
                            dve.wait_ge(st_mm, 2 * g + 2)
                            dve.wait_ge(dve_step, now)
                            dve.tensor_tensor(s1, s1, misc[:, :], ALU.add).then_inc(st1_ready, 1)
                        if i == 3:
                            dve.wait_ge(yo_mm, g + 1)
                            part = y3[:, :, 0:P]
                            dve.tensor_tensor(part, tp_b[:, :].rearrange("p (t i) -> p t i", t=GT),
                                              exps[:, :, 2 * NS + 2:EW], ALU.mult).then_inc(yo_read, 1)
                            dve.wait_ge(yo_read, g + 1)
                            dve.wait_ge(yd_read, 8 * g + 8)
                            dve.tensor_tensor(yt[:, :, P:SEQ], yt[:, :, P:SEQ], part, ALU.add).then_inc(dve_step, 1)
                            now = step()
                            dve.wait_ge(dve_step, now)
                            for t in range(GT):
                                dve.scalar_tensor_tensor(out=yt[:, t, 0:SEQ], in0=xbc[:, 2 + t, 0:SEQ],
                                                         scalar=exps[:, t, 2 * NS:2 * NS + 1], in1=yt[:, t, 0:SEQ],
                                                         op0=ALU.mult, op1=ALU.add).then_inc(dve_step, 1)
                                step()
                            sample_sum(g, 2)
                            dve.tensor_tensor(sml[:, 0], xbc_s[:, 2:CT], exps[:, :, 2 * NS:2 * NS + 1].to_broadcast(
                                [P, GT, NS]), ALU.mult).then_inc(dve_step, 1)
                            step()

            iteration(0, False)
            first, state["n"] = state["n"], 0
            per_group = first + 3
            with dve.Fori(1, G) as g:
                state["base"] = per_group * g - 3
                iteration(g, True)
            assert state["n"] == per_group
            state["base"], state["n"] = per_group * G - 3, 0
            rc = con[:, K_RC:K_RC + 16]

            def prompt_means(i, src):
                win, part = WINDOWS[i], poolu[:, 4 * i:4 * i + 4]
                wait(dve, phi_ready, i)
                wait(dve, plo_ready, i)
                dve.scalar_tensor_tensor(out=pp[:, :, 0:SEQ], in0=src[:, :, 16:16 + SEQ], scalar=1.0 / win,
                                         in1=part[:, :, 16:16 + SEQ], op0=ALU.mult, op1=ALU.subtract
                                         ).then_inc(dve_step, 1)
                few = win - 1
                small = psm[:, :, 0:few]
                dve.tensor_tensor(small, src[:, :, 16:16 + few], rc[:, 0:few].unsqueeze(1).to_broadcast([P, 4, few]),
                                  ALU.mult).then_inc(dve_step, 1)
                step()
                dve.wait_ge(dve_step, step())
                dve.tensor_tensor(pp[:, :, 0:few], small, part[:, :, 16:16 + few], ALU.subtract).then_inc(dve_step, 1)
                dve.wait_ge(dve_step, step())

            def sample_means(i):
                win, part = WINDOWS[i], poolu[:, 4 * i:4 * i + 4]
                if i == 0:
                    dve.wait_ge(spb_in, 16)
                    dve.tensor_copy(spb[:, :, :, POOL_BUF], poolu[:, :, 16 + SEQ:PW]).then_inc(pool_rows, 1)
                    dve.tensor_copy(ppo, poolu[:, :, 16 + SEQ - POOL_BUF:16 + SEQ]).then_inc(pool_rows, 1)
                    dve.wait_ge(pool_rows, 1)
                dve.tensor_reduce(psm[:, :, 16:16 + NS], spb[:, 4 * i:4 * i + 4, :, 16 - win:16], AX_X,
                                  ALU.add).then_inc(dve_step, 1)
                dve.wait_ge(dve_step, step())
                dve.scalar_tensor_tensor(out=pp[:, :, SEQ:T], in0=psm[:, :, 16:16 + NS], scalar=1.0 / win,
                                         in1=part[:, :, 16 + SEQ:PW], op0=ALU.mult, op1=ALU.subtract
                                         ).then_inc(pooled, 1)

            def low_of_pooled(i):
                dve.wait_ge(phi_ready, i + 1)
                dve.tensor_tensor(plo[i % 2], pp, phi[:, i % 2].bitcast(F32), ALU.subtract).then_inc(plo_ready, 1)

            early = [lambda h, j=j: split(Q_EARLY, 2 + 2 * j + h + RING) for j in range(4)]
            early[0](0)
            gate_y(G)
            early[0](1)
            early[1](0)
            normalise(G - 1, G)
            early[1](1)
            early[2](0)
            low_of_y(G)
            early[2](1)
            dve.wait_ge(conv_done, 24 * G)
            dve.wait_ge(ust_done, G)
            dve.wait_ge(pool_step, 9 * G - 8)
            prompt_means(0, window_sums(dve, 0, pa, pb, dve_step, step))
            early[3](0)
            early[3](1)
            for i in range(GT):
                branch(Q_TAIL, 2 + 2 * i, i, 0)
                if i == 0:
                    sample_means(0)
                    sums_1 = window_sums(dve, 1, pa, pb, dve_step, step)
                elif i == 1:
                    low_of_pooled(0)
                    prompt_means(1, sums_1)
                    sample_means(1)
                elif i == 2:
                    low_of_pooled(1)
                    sums_2 = window_sums(dve, 2, pa, pb, dve_step, step)
                else:
                    prompt_means(2, sums_2)
                    sample_means(2)
            for i in range(4):
                for h in range(2):
                    split(Q_POOL, 2 + 2 * i + h + RING)
                if i == 0:
                    low_of_pooled(2)
                    dve.wait_ge(widest_sum, 4)
                    prompt_means(3, qb)
                    sample_means(3)
                elif i == 1:
                    low_of_pooled(3)

            def mix(i, a):
                m, j = 2 * i + a, 2 * a
                dve.wait_ge(acc_act, ACT_GATE + 4 * i + j + 2)
                dve.tensor_tensor(mx[:, a, 0], sg[:, j], ya[:, m], ALU.mult).then_inc(mx_step, 1)
                dve.tensor_tensor(mx[:, a, 1], sg[:, j + 1], yb[:, m], ALU.mult).then_inc(mx_step, 1)
                dve.wait_ge(mx_step, 4 * i + 2 * a + 3)
                dve.tensor_tensor(mx[:, a, 0], mx[:, a, 0], mx[:, a, 1], ALU.add).then_inc(mx_ready, 1)
                dve.wait_ge(mhi_ready, m + 1)
                dve.tensor_tensor(mlo[:, m], mx[:, a, 0], mhi[:, m].bitcast(F32), ALU.subtract).then_inc(mlo_ready, 1)

            dve.memset(mx, 0.0).then_inc(mx_step, 1)
            dve.wait_ge(mx_step, 1)
            for a in range(2):
                mix(0, a)
            with dve.Fori(1, KT // 2) as i:
                for j in range(4):
                    for h in range(2):
                        split(Q_GATE + 2 * i, 2 + 2 * j + h + RING)
                    if j % 2:
                        mix(i, j // 2)

            def residual(bank, m, hi, lo, count):
                dve.scalar_tensor_tensor(out=res[:, m], in0=hi[:, m].bitcast(F32), scalar=ALPHA, in1=acc[bank][:, 0:T],
                                         op0=ALU.mult, op1=ALU.add).then_inc(acc_dve, 1)
                dve.wait_ge(acc_dve, count)
                dve.scalar_tensor_tensor(out=res[:, m], in0=lo[:, m].bitcast(F32), scalar=ALPHA, in1=res[:, m],
                                         op0=ALU.mult, op1=ALU.add).then_inc(res_ready, 1)

            with dve.Fori(0, KT // 4) as i:
                for j in range(4):
                    split(Q_OUT + 2 * i, 2 + 2 * j + RING)
                    dve.wait_ge(half_used, 4 * (Q_OUT + 2 * i) + 4 + 2 * j)
                    residual(j, 4 * i + j, xhi, xlo, DVE_OUT + 4 * i + j + 1)
                    split(Q_OUT + 2 * i, 2 + 2 * j + RING + 1)

            def low_of_even(m):
                dve.wait_ge(x1hi_ready, m + 1)
                dve.scalar_tensor_tensor(out=x1lo[:, m], in0=res[:, m], scalar=ln_column(0, 1, m),
                                         in1=x1hi[:, m].bitcast(F32), op0=ALU.add, op1=ALU.subtract
                                         ).then_inc(x1lo_even, 1)

            def layer_norm(n):
                def wide(row):
                    return lnr[:, row].unsqueeze(1).to_broadcast([P, 4, T])

                dve.wait_ge(mean_mm, n + 1)
                dve.wait_ge(res_ready, KT * (n + 1))
                dve.tensor_scalar(lnr[:, 0], seg_b[:, 0:T], 1.0 / D_MODEL, None, ALU.mult).then_inc(mu_ready, 1)
                dve.wait_ge(mu_ready, n + 1)
                for c in range(4):
                    part = res[:, 4 * c:4 * c + 4]
                    dve.tensor_tensor(part, part, wide(0), ALU.subtract).then_inc(rc_ready, 1)
                dve.wait_ge(sq_mm, 4 * n + 4)
                dve.tensor_scalar(lnr[:, 1], tp_b[:, 0:T], 1.0 / D_MODEL, EPS, ALU.mult, ALU.add).then_inc(var_ready, 1)
                dve.wait_ge(lnstd, n + 1)
                dve.reciprocal(lnr[:, 3], lnr[:, 2]).then_inc(lnr_ready, 1)
                dve.wait_ge(lnr_ready, n + 1)
                dve.wait_ge(rc_ready, 4 * n + 4)
                for m in range(0, KT, 2):
                    dve.scalar_tensor_tensor(out=res[:, m], in0=res[:, m], scalar=ln_column(n, 0, m), in1=lnr[:, 3],
                                             op0=ALU.mult, op1=ALU.mult).then_inc(even_normed, 1)
                    if n == 0 and m >= 4:
                        low_of_even(m - 4)
                    elif n == 1:
                        dve.wait_ge(even_normed, (KT + m) // 2 + 1)
                        dve.tensor_scalar(res[:, m], res[:, m], ln_column(1, 1, m), None, ALU.add).then_inc(y_even, 1)
                if n == 0:
                    for m in (KT - 4, KT - 2):
                        low_of_even(m)

            layer_norm(0)
            dve.memset(uf[:, :, 0:FFN_K - 1], 0.0).then_inc(fconv, 1)
            dve.wait_ge(fconv, 1)
            fc_s = fc[:, :, SEQ:FCW].rearrange("p w (b f) -> p w b f", f=FFN_K)

            def gated_product(j):
                dve.wait_ge(fsilu, j + 1)
                dve.wait_ge(fconv, 6 * j + 7)
                wait(dve, flo_ready, j)
                dve.tensor_tensor(hh[:, 0:SEQ], fc[:, 0, 0:SEQ], fc[:, 1, 0:SEQ], ALU.mult).then_inc(fh_ready, 1)
                dve.tensor_tensor(hh[:, SEQ:T], fc_s[:, 0, :, FFN_K - 1], fc_s[:, 1, :, FFN_K - 1],
                                  ALU.mult).then_inc(fh_ready, 1)

            def gated_low(j):
                dve.wait_ge(fhi_ready, j + 1)
                dve.tensor_tensor(hlo[:, j], hh, hhi[:, j].bitcast(F32), ALU.subtract).then_inc(flo_ready, 1)

            def up(j, first):
                for w in range(2):
                    split(Q_UP + j, 2 + 2 * w + RING)
                    if not first:
                        (gated_low if w else gated_product)(j - 1)
                    split(Q_UP + j, 2 + 2 * w + RING + 1)
                    dve.wait_ge(acc_act, ACT_UP + 2 * j + w + 1)
                    dve.wait_ge(fbuf_ready, j + 1)
                    wait(dve, fh_ready, 2 * j)
                    for k in range(FFN_K):
                        u, y = uf[:, w, k:k + FCW], fc[:, w]
                        if k == 0:
                            ins = dve.tensor_scalar(y, u, fc_w[:, j, w, 0:1], fc_w[:, j, w, FFN_K:FFN_K + 1],
                                                    ALU.mult, ALU.add)
                        else:
                            dve.wait_ge(fconv, 6 * j + 3 * w + k + 1)
                            ins = dve.scalar_tensor_tensor(out=y, in0=u, scalar=fc_w[:, j, w, k:k + 1], in1=y,
                                                           op0=ALU.mult, op1=ALU.add)
                        ins.then_inc(fconv, 1)

            up(0, True)
            with dve.Fori(1, JF) as j:
                up(j, False)
            gated_product(JF - 1)
            gated_low(JF - 1)

            def down(i, last):
                for j in range(4):
                    for n in range(6):
                        if not (last and j == 3 and n >= 2):
                            split(Q_DOWN + 6 * i, 2 + 6 * j + n + RING, DOWN_TILES[(n + RING) % 6])
                    dve.wait_ge(half_used, 4 * (Q_DOWN + 6 * i) + 2 + 6 * j + 6)
                    residual(j, 4 * i + j, x1hi, x1lo, DVE_DOWN + 4 * i + j + 1)

            with dve.Fori(0, KT // 4 - 1) as i:
                down(i, False)
            down(KT // 4 - 1, True)
            layer_norm(1)


def kernel(x_prompt, x_sample, state_ssm, state_ssd_conv, state_pool, state_ffn_conv, w_in, b_gate, conv_w, conv_b,
           dt_bias, a_log, d_skip, ssd_norm_w, w_ssd_branch, w_pool, pool_scale, w_out, ln1_g, ln1_b, w_up,
           ffn_conv_w, ffn_conv_b, w_down, ln2_g, ln2_b):
    import concourse.bacc as _bacc
    from concourse.bass_utils import run_bass_kernel_spmd as _run

    f32 = np.float32

    def arr(a):
        return np.asarray(a)

    def blocks(w, cols, k_tiles):
        w = w.reshape(k_tiles, P, -1)
        return np.stack([w[:, :, c:c + P].transpose(1, 0, 2).reshape(P, -1) for c in cols])

    def columns(v):
        return v.reshape(-1, P).T

    w_in, w_up, w_down = arr(w_in)[0], arr(w_up)[0], arr(w_down)[0]
    off_x, off_dt = D_INNER, 2 * D_INNER + 2 * G * D_STATE
    off_b = off_x + D_INNER
    off_pool, off_gate = off_dt + N_HEADS, off_dt + N_HEADS + D_MODEL
    group_cols = [[off_b + P * g, off_b + P * (G + g)] + [off_x + P * (GT * g + t) for t in range(GT)]
                  + [P * (GT * g + t) for t in range(GT)] + [off_pool + P * (2 * g + i) for i in range(2)]
                  for g in range(G)]
    conv_tiles = [[GT * G + g, GT * G + G + g] + [GT * g + t for t in range(GT)] for g in range(G)]
    x = np.concatenate([arr(x_prompt)[0], arr(x_sample)[:, 0]])

    cw = np.concatenate([arr(conv_w)[0], arr(conv_b)]).reshape(CONV_K + 1, -1, P)[:, conv_tiles]
    fcw = np.concatenate([arr(ffn_conv_w)[0], arr(ffn_conv_b)]).reshape(FFN_K + 1, 2, JF, P)
    heads = np.zeros((P, 3), f32)
    for i, v in enumerate((dt_bias, a_log, d_skip)):
        heads[:N_HEADS, i] = arr(v)[0]
    params = np.concatenate([
        cw.transpose(3, 1, 2, 0).reshape(P, -1), columns(arr(ssd_norm_w)[0]),
        arr(b_gate)[0].reshape(2, KT, P).transpose(2, 1, 0).reshape(P, -1), columns(arr(pool_scale)[0]),
        *(columns(arr(v)[0]) for v in (ln1_g, ln1_b, ln2_g, ln2_b)),
        fcw.transpose(3, 2, 1, 0).reshape(P, -1), heads], axis=1)

    r = np.arange(P)
    con = np.zeros((P, N_CON), f32)
    con[:, K_ID:K_ID + P] = r[:, None] == r[None, :]
    con[:, K_TRI:K_TRI + P] = r[:, None] <= r[None, :]
    con[:, K_LOW:K_LOW + P] = r[:, None] > r[None, :]
    con[:, K_ONE:K_ONE + P] = 1
    for t in range(GT):
        con[:N_HEADS, K_E + P * t:K_E + P * (t + 1)] = (r[:N_HEADS, None] % HG) == 2 * t + r[None, :] // HEAD_DIM
    con[:N_HEADS, K_MASK:K_MASK + G] = r[:N_HEADS, None] // HG == np.arange(G)
    con[:, K_RC:K_RC + 16] = f32(1) / np.arange(1, 17, dtype=f32)

    wb = arr(w_ssd_branch)[0].reshape(G, GT, P, 4, GT, P)
    wp = arr(w_pool)[0].reshape(4, 4, P, 4, P)
    st = arr(state_ssm)[0].reshape(4, 2, G, GT, P, D_STATE)
    arrays = {
        "x": x.reshape(T, KT, P).transpose(2, 1, 0),
        "w_dt": blocks(w_in, [off_dt], KT)[0],
        "w_in": np.stack([blocks(w_in, c, KT) for c in group_cols]),
        "w_branch": wb.transpose(0, 3, 2, 4, 1, 5).reshape(G, 4, P, -1),
        "w_pool": wp.transpose(0, 2, 3, 1, 4).reshape(4, P, -1),
        "w_gate": blocks(w_in, [off_gate + D_MODEL * h + P * m for m in range(KT) for h in range(2)], KT),
        "w_out": blocks(arr(w_out)[0], [P * m for m in range(KT)], KT),
        "w_up": blocks(w_up, [D_FF * h + P * j for j in range(JF) for h in range(2)], KT).reshape(JF, 2, P, -1),
        "w_down": blocks(w_down, [P * m for m in range(KT)], JF),
        "constants": con,
        "params": params,
        "state": st.transpose(2, 0, 4, 1, 3, 5).reshape(G, 4, P, -1),
        "conv_rows": arr(state_ssd_conv)[0].reshape(NS, 3, -1, P)[:, :, conv_tiles].transpose(4, 2, 3, 0, 1),
        "pool_rows": np.concatenate([arr(state_pool)[0], np.zeros((NS, 1, D_MODEL), f32)], axis=1)
        .reshape(NS, 16, KT, P).transpose(3, 2, 0, 1),
        "ffn_rows": arr(state_ffn_conv)[0].reshape(NS, 2, 2, JF, P).transpose(4, 3, 2, 0, 1),
    }
    outs = {
        "y": (P, KT, T), "ssm_p": (G, P, GT * P), "conv_p": (P, G, CT, 3), "pool_p": (P, KT, POOL_BUF),
        "ffn_p": (P, JF, 2, 2), "ssm_s": (G, 4, P, 2 * GT * P), "conv_s": (P, G, CT, NS, 3),
        "pool_s": (P, KT, NS, 16), "ffn_s": (P, JF, 2, NS, 2),
    }
    nc = _bacc.Bacc("TRN2", target_bir_lowering=False, num_devices=1, dynamic_dma_scratch_size=4096)
    arrays = {k: np.ascontiguousarray(v) for k, v in arrays.items()}
    A = {k: nc.dram_tensor(f"in_{k}", v.shape, F32, kind="ExternalInput").ap() for k, v in arrays.items()}
    O = {k: nc.dram_tensor(f"out_{k}", s, F32, kind="ExternalOutput").ap() for k, s in outs.items()}
    bass_hybrid_layer(nc, A, O)
    r = _run(nc, [{f"in_{k}": v for k, v in arrays.items()}], core_ids=[0]).results[0]
    r = {k: r[f"out_{k}"] for k in outs}

    y = r["y"].transpose(2, 1, 0).reshape(T, D_MODEL)

    def conv_rows(a):
        a = np.moveaxis(a, 0, -1)
        rows = a.shape[2:-1]
        parts = [a[:, 2:].reshape(G * GT, *rows, P), a[:, 0], a[:, 1]]
        a = np.concatenate(parts)
        return np.moveaxis(a, 0, -2).reshape(*rows, -1)

    return (
        y[:SEQ][None], y[SEQ:][:, None],
        r["ssm_p"].transpose(0, 2, 1).reshape(1, 1, N_HEADS, HEAD_DIM, D_STATE),
        conv_rows(r["conv_p"])[None, None],
        r["pool_p"].transpose(2, 1, 0).reshape(1, 1, POOL_BUF, D_MODEL),
        r["ffn_p"].transpose(3, 2, 1, 0).reshape(1, 1, 2, 2 * D_FF),
        r["ssm_s"].reshape(G, 4, P, 2, GT, D_STATE).transpose(1, 3, 0, 4, 2, 5)
        .reshape(1, NS, N_HEADS, HEAD_DIM, D_STATE),
        conv_rows(r["conv_s"])[None],
        r["pool_s"][:, :, :, 1:].transpose(2, 3, 1, 0).reshape(1, NS, POOL_BUF, D_MODEL),
        r["ffn_s"].transpose(3, 4, 2, 1, 0).reshape(1, NS, 2, 2 * D_FF),
    )
```
